# Optimizing a Trainium2 kernel written in Bass

```python
import jax, jax.numpy as jnp
from jax import lax
import numpy as np

D_MODEL = 1024
BATCH = 1
SEQ = 256
DEPTH = 1

CTX_LEN = 256
GRID_W = 64

GLA_HEADS = 4
GLA_DK = 128
GLA_DV = 256
GLA_RANK = 16
GLA_TAU = 16.0
GLA_CHUNK = 64
GLA_QK = GLA_HEADS * GLA_DK
GLA_V = GLA_HEADS * GLA_DV

RET_HEADS = 4
RET_DK = 128
RET_DV = 256
RET_CHUNK = 128
RET_QK = RET_HEADS * RET_DK
RET_V = RET_HEADS * RET_DV
ROPE_BASE = 10000.0

N_GROUPS = 4
EXPERTS_PER_GROUP = 8
N_EXPERTS = N_GROUPS * EXPERTS_PER_GROUP
TOP_K = 2
EXPERT_FF = 256
MOE_BLOCK = 128

NORM_EPS = 1e-6

IN_SPLITS = (GLA_QK, GLA_QK, GLA_V, GLA_V, GLA_RANK, GLA_RANK,
             RET_QK, RET_QK, RET_V, RET_V, D_MODEL, D_MODEL)
IN_WIDTH = sum(IN_SPLITS)


def rmsnorm(x, g):
    xf = x.astype(jnp.float32)
    y = xf * lax.rsqrt(jnp.mean(xf * xf, axis=-1, keepdims=True) + NORM_EPS)
    return (y * g.astype(jnp.float32)).astype(x.dtype)

def head_groupnorm(o):
    of = o.astype(jnp.float32)
    mu = jnp.mean(of, axis=-1, keepdims=True)
    var = jnp.mean(jnp.square(of - mu), axis=-1, keepdims=True)
    return ((of - mu) * lax.rsqrt(var + NORM_EPS)).astype(o.dtype)

def modulate(h, shift, scale):
    return h * (1.0 + scale) + shift

def split_columns(proj):
    out = []
    start = 0
    for w in IN_SPLITS:
        out.append(proj[..., start:start + w])
        start += w
    return out

def retention_log_decays():
    h = jnp.arange(RET_HEADS, dtype=jnp.float32)
    fwd = jnp.log1p(-jnp.exp2(-5.0 - h))
    bwd = jnp.log1p(-jnp.exp2(-5.5 - h))
    return fwd, bwd

def axial_rope(t, rows, cols):
    half = t.shape[-1] // 2
    n = half // 2
    inv = ROPE_BASE ** (-jnp.arange(n, dtype=jnp.float32) / n)

    def rot(u, p):
        ang = p[:, None] * inv[None, :]
        cos = jnp.cos(ang)[None, :, None, :].astype(u.dtype)
        sin = jnp.sin(ang)[None, :, None, :].astype(u.dtype)
        u1, u2 = u[..., :n], u[..., n:]
        return jnp.concatenate([u1 * cos - u2 * sin, u1 * sin + u2 * cos], axis=-1)

    return jnp.concatenate([rot(t[..., :half], rows), rot(t[..., half:], cols)], axis=-1)

def to_chunks(t, chunk):
    B, L, H, W = t.shape
    return jnp.moveaxis(t.reshape(B, L // chunk, chunk, H, W), 1, 0)

def from_chunks(o):
    N, B, C, H, W = o.shape
    return jnp.moveaxis(o, 0, 1).reshape(B, N * C, H, W)

def gla_scan(q, k, v, log_a, s0, strict):
    C = GLA_CHUNK
    ti = jnp.arange(C)
    mask = (ti[:, None] > ti[None, :]) if strict else (ti[:, None] >= ti[None, :])
    mask5 = mask[None, :, :, None, None]

    def step(S, inp):
        qc, kc, vc, lac = inp
        b = jnp.cumsum(lac.astype(jnp.float32), axis=1)
        inter = jnp.einsum('bthk,bhkv->bthv', qc * jnp.exp(b), S)
        decay = jnp.exp(jnp.where(mask5, b[:, :, None] - b[:, None, :], -jnp.inf))
        scores = jnp.einsum('bthk,btshk,bshk->btsh', qc, decay, kc)
        intra = jnp.einsum('btsh,bshv->bthv', scores, vc)
        b_last = b[:, -1]
        S_new = jnp.exp(b_last)[..., None] * S + jnp.einsum(
            'bshk,bshv->bhkv', kc * jnp.exp(b_last[:, None] - b), vc)
        return S_new, inter + intra

    S_fin, o = lax.scan(step, s0, (to_chunks(q, C), to_chunks(k, C), to_chunks(v, C), to_chunks(log_a, C)))
    return from_chunks(o).astype(v.dtype), S_fin

def retention_scan(q, k, v, log_gamma, s0, strict):
    C = RET_CHUNK
    pos = jnp.arange(C, dtype=jnp.float32)
    ti = jnp.arange(C)
    mask = (ti[:, None] > ti[None, :]) if strict else (ti[:, None] >= ti[None, :])
    rel = pos[:, None] - pos[None, :]
    dmat = jnp.exp(jnp.where(mask[None], rel[None] * log_gamma[:, None, None], -jnp.inf))
    q_decay = jnp.exp((pos + 1.0)[:, None] * log_gamma[None, :])
    k_decay = jnp.exp((C - 1.0 - pos)[:, None] * log_gamma[None, :])
    c_decay = jnp.exp(C * log_gamma)

    def step(S, inp):
        qc, kc, vc = inp
        inter = jnp.einsum('bthk,bhkv->bthv', qc, S) * q_decay[None, :, :, None]
        scores = jnp.einsum('bthk,bshk->bhts', qc, kc) * dmat[None]
        intra = jnp.einsum('bhts,bshv->bthv', scores, vc)
        S_new = c_decay[None, :, None, None] * S + jnp.einsum(
            'bshk,bshv->bhkv', kc * k_decay[None, :, :, None], vc)
        return S_new, inter + intra

    S_fin, o = lax.scan(step, s0, (to_chunks(q, C), to_chunks(k, C), to_chunks(v, C)))
    return from_chunks(o).astype(v.dtype), S_fin

def mixer_heads(h, w_in, gla_lr_w, gla_lr_b, gla_norm, states, rope):
    B, L, _ = h.shape
    (gq, gk, gv, gg, glr_f, glr_b, rq, rk, rv, rg, m_gla, m_ret) = split_columns(h @ w_in)

    def heads(t, n):
        return t.reshape(B, L, n, -1)

    def flip(t):
        return jnp.flip(t, axis=1)

    gq = heads(gq, GLA_HEADS) * GLA_DK ** -0.5
    gk = heads(gk, GLA_HEADS)
    gv = heads(gv, GLA_HEADS)

    def log_gate(lr, d):
        z = (lr @ gla_lr_w[d] + gla_lr_b[d]).astype(jnp.float32)
        return heads(jax.nn.log_sigmoid(z) / GLA_TAU, GLA_HEADS)

    o_f, s_gf = gla_scan(gq, gk, gv, log_gate(glr_f, 0), states[0], False)
    o_b, s_gb = gla_scan(flip(gq), flip(gk), flip(gv), flip(log_gate(glr_b, 1)), states[1], True)
    o_gla = rmsnorm(o_f + flip(o_b), gla_norm) * jax.nn.silu(heads(gg, GLA_HEADS))
    o_gla = o_gla.reshape(B, L, GLA_V)

    rq = heads(rq, RET_HEADS)
    rk = heads(rk, RET_HEADS) * RET_DK ** -0.5
    rv = heads(rv, RET_HEADS)
    if rope is not None:
        rq = axial_rope(rq, rope[0], rope[1])
        rk = axial_rope(rk, rope[0], rope[1])
    lg_f, lg_b = retention_log_decays()
    r_f, s_rf = retention_scan(rq, rk, rv, lg_f, states[2], False)
    r_b, s_rb = retention_scan(flip(rq), flip(rk), flip(rv), lg_b, states[3], True)
    o_ret = head_groupnorm(r_f + flip(r_b)) * jax.nn.silu(heads(rg, RET_HEADS))
    o_ret = o_ret.reshape(B, L, RET_V)
    return o_gla, o_ret, m_gla, m_ret, (s_gf, s_gb, s_rf, s_rb)

def merge_branches(o_gla, o_ret, m_gla, m_ret, w_branch_gla, w_branch_ret, w_out):
    y = jax.nn.sigmoid(m_gla) * (o_gla @ w_branch_gla) + jax.nn.sigmoid(m_ret) * (o_ret @ w_branch_ret)
    return y @ w_out

def hier_moe(h, w_rg, b_rg, w_re, b_re, w_gate, w_up, w_down):
    B, L, D = h.shape
    T = B * L
    xt = h.reshape(T, D)
    g_logits = (xt @ w_rg + b_rg).astype(jnp.float32)
    g_prob = jax.nn.softmax(g_logits, axis=-1)
    g_sel = jnp.argmax(g_logits, axis=-1).astype(jnp.int32)
    g_w = jnp.take_along_axis(g_prob, g_sel[:, None], axis=-1)[:, 0]
    e_logits = (xt @ w_re + b_re).astype(jnp.float32).reshape(T, N_GROUPS, EXPERTS_PER_GROUP)
    e_logits = jnp.take_along_axis(e_logits, g_sel[:, None, None], axis=1)[:, 0]
    top_v, top_i = lax.top_k(e_logits, TOP_K)
    e_w = jax.nn.softmax(top_v, axis=-1) * g_w[:, None]
    expert_id = g_sel[:, None] * EXPERTS_PER_GROUP + top_i.astype(jnp.int32)

    A = T * TOP_K
    flat_e = expert_id.reshape(A)
    flat_tok = jnp.repeat(jnp.arange(T, dtype=jnp.int32), TOP_K)
    flat_w = e_w.reshape(A)
    order = jnp.argsort(flat_e)
    se, stok, sw = flat_e[order], flat_tok[order], flat_w[order]
    counts = jax.ops.segment_sum(jnp.ones((A,), jnp.int32), flat_e, num_segments=N_EXPERTS)
    starts = jnp.cumsum(counts) - counts
    padded = (counts + MOE_BLOCK - 1) // MOE_BLOCK * MOE_BLOCK
    pends = jnp.cumsum(padded)
    pstarts = pends - padded
    dest = pstarts[se] + jnp.arange(A, dtype=jnp.int32) - starts[se]
    P = A + N_EXPERTS * MOE_BLOCK
    NB = P // MOE_BLOCK
    x_pad = jnp.zeros((P, D), h.dtype).at[dest].set(xt[stok])
    tok_pad = jnp.zeros((P,), jnp.int32).at[dest].set(stok)
    w_pad = jnp.zeros((P,), jnp.float32).at[dest].set(sw)
    block_start = jnp.arange(NB, dtype=jnp.int32) * MOE_BLOCK
    block_e = jnp.minimum(jnp.searchsorted(pends, block_start, side='right'), N_EXPERTS - 1)

    def expert_block(args):
        xb, e = args
        hid = jax.nn.silu(xb @ w_gate[e]) * (xb @ w_up[e])
        return hid @ w_down[e]

    y = lax.map(expert_block, (x_pad.reshape(NB, MOE_BLOCK, D), block_e)).reshape(P, D)
    out = jnp.zeros((T, D), jnp.float32).at[tok_pad].add(y.astype(jnp.float32) * w_pad[:, None])
    return out.astype(h.dtype).reshape(B, L, D)

def first_inputs(seed: int = 0) -> dict:
    key = jax.random.key(seed)
    ks = jax.random.split(key, 24)

    def nrm(k, shape, scale):
        return jax.random.normal(k, shape, jnp.float32) * scale

    D = D_MODEL
    return {
        'x': nrm(ks[0], (BATCH, SEQ, D), 1.0),
        'c': nrm(ks[1], (BATCH, D), 1.0),
        'ctx': nrm(ks[2], (BATCH, CTX_LEN, D), 1.0),
        'c_ctx': nrm(ks[3], (D,), 1.0),
        'w_ada': nrm(ks[4], (DEPTH, D, 6 * D), D ** -0.5),
        'b_ada': nrm(ks[5], (DEPTH, 6 * D), 0.02),
        'norm_mix': 1.0 + nrm(ks[6], (DEPTH, D), 0.05),
        'norm_ffn': 1.0 + nrm(ks[7], (DEPTH, D), 0.05),
        'w_in': nrm(ks[8], (DEPTH, D, IN_WIDTH), D ** -0.5),
        'gla_lr_w': nrm(ks[9], (DEPTH, 2, GLA_RANK, GLA_QK), GLA_RANK ** -0.5),
        'gla_lr_b': nrm(ks[10], (DEPTH, 2, GLA_QK), 0.1),
        'gla_norm': 1.0 + nrm(ks[11], (DEPTH, GLA_DV), 0.05),
        'w_branch_gla': nrm(ks[12], (DEPTH, GLA_V, D), GLA_V ** -0.5),
        'w_branch_ret': nrm(ks[13], (DEPTH, RET_V, D), RET_V ** -0.5),
        'w_out': nrm(ks[14], (DEPTH, D, D), D ** -0.5),
        'w_router_group': nrm(ks[15], (DEPTH, D, N_GROUPS), D ** -0.5),
        'b_router_group': nrm(ks[16], (DEPTH, N_GROUPS), 0.01),
        'w_router_expert': nrm(ks[17], (DEPTH, D, N_EXPERTS), D ** -0.5),
        'b_router_expert': nrm(ks[18], (DEPTH, N_EXPERTS), 0.01),
        'w_expert_gate': nrm(ks[19], (DEPTH, N_EXPERTS, D, EXPERT_FF), D ** -0.5),
        'w_expert_up': nrm(ks[20], (DEPTH, N_EXPERTS, D, EXPERT_FF), D ** -0.5),
        'w_expert_down': nrm(ks[21], (DEPTH, N_EXPERTS, EXPERT_FF, D), EXPERT_FF ** -0.5),
        'norm_final': 1.0 + nrm(ks[22], (D,), 0.05),
    }

def first_block(x, c, ctx, c_ctx, w_ada, b_ada, norm_mix, norm_ffn, w_in, gla_lr_w, gla_lr_b, gla_norm,
              w_branch_gla, w_branch_ret, w_out, w_router_group, b_router_group, w_router_expert,
              b_router_expert, w_expert_gate, w_expert_up, w_expert_down, norm_final):
    B, L, _ = x.shape
    ROWS = L // GRID_W
    rows = jnp.repeat(jnp.arange(ROWS, dtype=jnp.float32), GRID_W)
    cols = jnp.tile(jnp.arange(GRID_W, dtype=jnp.float32), ROWS)
    zero_states = (
        jnp.zeros((B, GLA_HEADS, GLA_DK, GLA_DV), jnp.float32),
        jnp.zeros((B, GLA_HEADS, GLA_DK, GLA_DV), jnp.float32),
        jnp.zeros((B, RET_HEADS, RET_DK, RET_DV), jnp.float32),
        jnp.zeros((B, RET_HEADS, RET_DK, RET_DV), jnp.float32),
    )
    h_lat = x
    h_ctx = ctx
    for layer in range(DEPTH):
        sh1, sc1, g1, sh2, sc2, g2 = jnp.split(
            (jax.nn.silu(c) @ w_ada[layer] + b_ada[layer])[:, None, :], 6, axis=-1)
        csh1, csc1, cg1, csh2, csc2, cg2 = jnp.split(
            (jax.nn.silu(c_ctx) @ w_ada[layer] + b_ada[layer])[None, None, :], 6, axis=-1)
        mix_args = (w_in[layer], gla_lr_w[layer], gla_lr_b[layer], gla_norm[layer])
        merge_args = (w_branch_gla[layer], w_branch_ret[layer], w_out[layer])
        moe_args = (w_router_group[layer], b_router_group[layer], w_router_expert[layer],
                    b_router_expert[layer], w_expert_gate[layer], w_expert_up[layer], w_expert_down[layer])

        hc = modulate(rmsnorm(h_ctx, norm_mix[layer]), csh1, csc1)
        c_gla, c_ret, c_mg, c_mr, ctx_states = mixer_heads(hc, *mix_args, zero_states, None)

        hl = modulate(rmsnorm(h_lat, norm_mix[layer]), sh1, sc1)
        l_gla, l_ret, l_mg, l_mr, _ = mixer_heads(hl, *mix_args, ctx_states, (rows, cols))
        h_lat = h_lat + g1 * merge_branches(l_gla, l_ret, l_mg, l_mr, *merge_args)
        h_lat = h_lat + g2 * hier_moe(modulate(rmsnorm(h_lat, norm_ffn[layer]), sh2, sc2), *moe_args)

        if layer < DEPTH - 1:
            h_ctx = h_ctx + cg1 * merge_branches(c_gla, c_ret, c_mg, c_mr, *merge_args)
            h_ctx = h_ctx + cg2 * hier_moe(modulate(rmsnorm(h_ctx, norm_ffn[layer]), csh2, csc2), *moe_args)
    return rmsnorm(h_lat, norm_final)


HEAD_DIM = 64
ROPE_THETA = 10000.0
EPS = 1e-6
ATTN_SCALE = HEAD_DIM ** -0.5
Q_BLOCK = 128

DSA_HEADS = 8
DSA_Q_RANK = 256
DSA_KV_RANK = 128
IDX_HEADS = 8
IDX_DIM = 64
IDX_SCALE = IDX_HEADS ** -0.5 * IDX_DIM ** -0.5
DSA_TOPK_MAX = 256

NSA_HEADS = 8
NSA_KV_HEADS = 2
NSA_GROUP = NSA_HEADS // NSA_KV_HEADS
CMP_BLOCK = 32
CMP_STRIDE = 16
SLC_BLOCK = 64
SLC_COUNT = 16
WINDOW = 512
FORCE_BONUS = 1e4

MIX_WIDTH = DSA_HEADS * HEAD_DIM + NSA_HEADS * HEAD_DIM
IN_SIZES = (DSA_Q_RANK, DSA_KV_RANK, IDX_DIM, IDX_HEADS,
            NSA_HEADS * HEAD_DIM, 3 * 2 * NSA_KV_HEADS * HEAD_DIM, NSA_HEADS * 3)
IN_WIDTH_2 = sum(IN_SIZES)

MEM_LEN = 256
XATTN_HEADS = 4
XATTN_HEAD_DIM = 128

D_FF = 4 * D_MODEL


def _rms_norm(x, g):
    xf = x.astype(jnp.float32)
    y = xf * lax.rsqrt(jnp.mean(xf * xf, axis=-1, keepdims=True) + EPS)
    return (y * g.astype(jnp.float32)).astype(x.dtype)

def _layer_norm(x, g, b):
    xf = x.astype(jnp.float32)
    mu = jnp.mean(xf, axis=-1, keepdims=True)
    var = jnp.mean(jnp.square(xf - mu), axis=-1, keepdims=True)
    y = (xf - mu) * lax.rsqrt(var + EPS) * g.astype(jnp.float32) + b.astype(jnp.float32)
    return y.astype(x.dtype)

def _rope(x, pos):
    half = x.shape[-1] // 2
    inv = ROPE_THETA ** (-jnp.arange(half, dtype=jnp.float32) / half)
    ang = pos.astype(jnp.float32)[:, None] * inv[None, :]
    cos = jnp.cos(ang)[:, None, :]
    sin = jnp.sin(ang)[:, None, :]
    xf = x.astype(jnp.float32)
    x1, x2 = xf[..., :half], xf[..., half:]
    return jnp.concatenate([x1 * cos - x2 * sin, x1 * sin + x2 * cos], axis=-1).astype(x.dtype)

def _masked_softmax(s, mask):
    s = jnp.where(mask, s, -jnp.inf)
    m = jnp.max(s, axis=-1, keepdims=True)
    m = jnp.where(jnp.isfinite(m), m, 0.0)
    p = jnp.where(mask, jnp.exp(s - m), 0.0)
    return p / jnp.maximum(jnp.sum(p, axis=-1, keepdims=True), 1e-30)

def _hybrid_mixer(h, w_in, dsa_cq_g, dsa_ckv_g, w_dsa_uq, w_dsa_ukv, w_idx_q, idx_k_ln_g, idx_k_ln_b,
                  dsa_qn_g, dsa_kn_g, nsa_cmp_pe, w_nsa_cmp, nsa_qn_g, nsa_kn_g, w_out):
    B, L, _ = h.shape
    G, R, D = NSA_KV_HEADS, NSA_GROUP, HEAD_DIM
    pos = jnp.arange(L, dtype=jnp.int32)
    splits = [int(v) for v in np.cumsum(IN_SIZES)[:-1]]
    proj = h @ w_in
    c_q, c_kv, k_idx, w_idx, q_nsa, kv_nsa, g_nsa = jnp.split(proj, splits, axis=-1)

    c_q = _rms_norm(c_q, dsa_cq_g)
    c_kv = _rms_norm(c_kv, dsa_ckv_g)
    q_d = _rope(_rms_norm((c_q @ w_dsa_uq).reshape(B, L, DSA_HEADS, D), dsa_qn_g), pos)
    k_d, v_d = jnp.split(c_kv @ w_dsa_ukv, 2, axis=-1)
    k_d = _rope(_rms_norm(k_d, dsa_kn_g)[:, :, None, :], pos)[:, :, 0, :]
    q_i = _rope((c_q @ w_idx_q).reshape(B, L, IDX_HEADS, IDX_DIM), pos)
    k_i = _rope(_layer_norm(k_idx, idx_k_ln_g, idx_k_ln_b)[:, :, None, :], pos)[:, :, 0, :]
    w_i = w_idx * IDX_SCALE
    k_dsa = min(DSA_TOPK_MAX, L // 4)

    q_n = _rope(_rms_norm(q_nsa.reshape(B, L, NSA_HEADS, D), nsa_qn_g), pos)
    kv = kv_nsa.reshape(B, L, 3, 2, G, D)
    k_br, v_br = kv[:, :, :, 0], kv[:, :, :, 1]
    k_slc = _rope(_rms_norm(k_br[:, :, 1], nsa_kn_g[1]), pos)
    k_win = _rope(_rms_norm(k_br[:, :, 2], nsa_kn_g[2]), pos)
    v_slc, v_win = v_br[:, :, 1], v_br[:, :, 2]

    n_cmp = (L - CMP_BLOCK) // CMP_STRIDE + 1
    tok = jnp.arange(n_cmp)[:, None] * CMP_STRIDE + jnp.arange(CMP_BLOCK)[None, :]
    cmp_end = tok[:, -1]
    k_blocks = k_br[:, :, 0][:, tok] + nsa_cmp_pe[0][:, None, :]
    v_blocks = v_br[:, :, 0][:, tok] + nsa_cmp_pe[1][:, None, :]
    k_c = jnp.einsum('bnlgd,lde->bnge', k_blocks, w_nsa_cmp[0])
    v_c = jnp.einsum('bnlgd,lde->bnge', v_blocks, w_nsa_cmp[1])
    k_c = _rope(_rms_norm(k_c, nsa_kn_g[0]), cmp_end)

    n_slc = L // SLC_BLOCK
    n_sel = min(SLC_COUNT, n_slc)
    ci = jnp.arange(n_cmp)[:, None] * CMP_STRIDE
    sj = jnp.arange(n_slc)[None, :] * SLC_BLOCK
    overlap = ((ci < sj + SLC_BLOCK) & (ci + CMP_BLOCK > sj)).astype(jnp.float32)
    k_slc_blk = k_slc.reshape(B, n_slc, SLC_BLOCK, G, D).transpose(0, 3, 1, 2, 4)
    v_slc_blk = v_slc.reshape(B, n_slc, SLC_BLOCK, G, D).transpose(0, 3, 1, 2, 4)

    k_win_pad = jnp.pad(k_win, ((0, 0), (WINDOW, 0), (0, 0), (0, 0)))
    v_win_pad = jnp.pad(v_win, ((0, 0), (WINDOW, 0), (0, 0), (0, 0)))

    gates = jax.nn.sigmoid(g_nsa.astype(jnp.float32)).astype(h.dtype).reshape(B, L, NSA_HEADS, 3)

    n_qb = L // Q_BLOCK

    def blocks(a):
        return jnp.moveaxis(a.reshape((B, n_qb, Q_BLOCK) + a.shape[2:]), 1, 0)

    bidx3 = jnp.arange(B)[:, None, None]
    bidx4 = jnp.arange(B)[:, None, None, None]
    gidx4 = jnp.arange(G)[None, :, None, None]
    j_slc = jnp.arange(n_slc)

    def step(args):
        qb, qd, qi, wi, qn, gt = args
        t = qb * Q_BLOCK + jnp.arange(Q_BLOCK, dtype=jnp.int32)

        idx_score = jnp.einsum('bqhs,bqh->bqs',
                               jax.nn.relu(jnp.einsum('bqhd,bsd->bqhs', qi, k_i)), wi).astype(jnp.float32)
        idx_score = jnp.where(pos[None, None, :] <= t[None, :, None], idx_score, -jnp.inf)
        _, sel = lax.top_k(idx_score, k_dsa)
        kg = k_d[bidx3, sel]
        vg = v_d[bidx3, sel]
        s = jnp.einsum('bqhd,bqkd->bhqk', qd, kg).astype(jnp.float32) * ATTN_SCALE
        p = _masked_softmax(s, (sel <= t[None, :, None])[:, None])
        o_dsa = jnp.einsum('bhqk,bqkd->bqhd', p.astype(vg.dtype), vg)

        qg = qn.reshape(B, Q_BLOCK, G, R, D)
        s = jnp.einsum('bqgrd,bngd->bgrqn', qg, k_c).astype(jnp.float32) * ATTN_SCALE
        p_cmp = _masked_softmax(s, cmp_end[None, :] <= t[:, None])
        o_cmp = jnp.einsum('bgrqn,bngd->bqgrd', p_cmp.astype(v_c.dtype), v_c)
        blk_score = jnp.einsum('bgrqn,nj->bgqj', p_cmp, overlap)
        tb = t // SLC_BLOCK
        forced = (j_slc[None, :] == 0) | (j_slc[None, :] == tb[:, None]) | (j_slc[None, :] == tb[:, None] - 1)
        admissible = j_slc[None, :] * SLC_BLOCK <= t[:, None]
        blk_score = jnp.where(admissible, blk_score + jnp.where(forced, FORCE_BONUS, 0.0), -jnp.inf)
        _, sel_blk = lax.top_k(blk_score, n_sel)
        kb = k_slc_blk[bidx4, gidx4, sel_blk].reshape(B, G, Q_BLOCK, n_sel * SLC_BLOCK, D)
        vb = v_slc_blk[bidx4, gidx4, sel_blk].reshape(B, G, Q_BLOCK, n_sel * SLC_BLOCK, D)
        kpos = (sel_blk[..., None] * SLC_BLOCK + jnp.arange(SLC_BLOCK)).reshape(B, G, Q_BLOCK, n_sel * SLC_BLOCK)
        s = jnp.einsum('bqgrd,bgqkd->bgrqk', qg, kb).astype(jnp.float32) * ATTN_SCALE
        p = _masked_softmax(s, (kpos <= t[None, None, :, None])[:, :, None])
        o_slc = jnp.einsum('bgrqk,bgqkd->bqgrd', p.astype(vb.dtype), vb)
        kw = lax.dynamic_slice_in_dim(k_win_pad, qb * Q_BLOCK, WINDOW + Q_BLOCK, axis=1)
        vw = lax.dynamic_slice_in_dim(v_win_pad, qb * Q_BLOCK, WINDOW + Q_BLOCK, axis=1)
        wpos = qb * Q_BLOCK - WINDOW + jnp.arange(WINDOW + Q_BLOCK, dtype=jnp.int32)
        wmask = (wpos[None, :] <= t[:, None]) & (wpos[None, :] > t[:, None] - WINDOW) & (wpos[None, :] >= 0)
        s = jnp.einsum('bqgrd,bkgd->bgrqk', qg, kw).astype(jnp.float32) * ATTN_SCALE
        p = _masked_softmax(s, wmask)
        o_win = jnp.einsum('bgrqk,bkgd->bqgrd', p.astype(vw.dtype), vw)
        gt = gt.reshape(B, Q_BLOCK, G, R, 3)
        o_nsa = o_cmp * gt[..., 0:1] + o_slc * gt[..., 1:2] + o_win * gt[..., 2:3]

        return jnp.concatenate([o_dsa.reshape(B, Q_BLOCK, -1), o_nsa.reshape(B, Q_BLOCK, -1)], axis=-1)

    xs = (jnp.arange(n_qb, dtype=jnp.int32), blocks(q_d), blocks(q_i), blocks(w_i), blocks(q_n), blocks(gates))
    o = lax.map(step, xs)
    o = jnp.moveaxis(o, 0, 1).reshape(B, L, MIX_WIDTH)
    return o @ w_out

def _memory_xattn(h, mem, mem_norm_g, w_xq, w_xk, w_xv, xq_norm_g, xk_norm_g, w_xo):
    B, L, _ = h.shape
    M = mem.shape[1]
    m = _rms_norm(mem, mem_norm_g)
    q = _rms_norm((h @ w_xq).reshape(B, L, XATTN_HEADS, XATTN_HEAD_DIM), xq_norm_g)
    k = _rms_norm((m @ w_xk).reshape(B, M, XATTN_HEADS, XATTN_HEAD_DIM), xk_norm_g)
    v = (m @ w_xv).reshape(B, M, XATTN_HEADS, XATTN_HEAD_DIM)
    s = jnp.einsum('bqhd,bmhd->bhqm', q, k).astype(jnp.float32) * (XATTN_HEAD_DIM ** -0.5)
    p = jax.nn.softmax(s, axis=-1).astype(v.dtype)
    o = jnp.einsum('bhqm,bmhd->bqhd', p, v).reshape(B, L, XATTN_HEADS * XATTN_HEAD_DIM)
    return o @ w_xo

def _sq_relu_mlp(h, w_ff_in, w_ff_out):
    return jnp.square(jax.nn.relu(h @ w_ff_in)) @ w_ff_out

def second_inputs(seed: int = 0) -> dict:
    key = jax.random.key(seed)
    D = HEAD_DIM
    specs = [
        ("norm1_g", (D_MODEL,), "g", 1),
        ("w_in", (D_MODEL, IN_WIDTH_2), "w", D_MODEL),
        ("dsa_cq_g", (DSA_Q_RANK,), "g", 1),
        ("dsa_ckv_g", (DSA_KV_RANK,), "g", 1),
        ("w_dsa_uq", (DSA_Q_RANK, DSA_HEADS * D), "w", DSA_Q_RANK),
        ("w_dsa_ukv", (DSA_KV_RANK, 2 * D), "w", DSA_KV_RANK),
        ("w_idx_q", (DSA_Q_RANK, IDX_HEADS * IDX_DIM), "w", DSA_Q_RANK),
        ("idx_k_ln_g", (IDX_DIM,), "g", 1),
        ("idx_k_ln_b", (IDX_DIM,), "b", 1),
        ("dsa_qn_g", (D,), "g", 1),
        ("dsa_kn_g", (D,), "g", 1),
        ("nsa_cmp_pe", (2, CMP_BLOCK, D), "b", 1),
        ("w_nsa_cmp", (2, CMP_BLOCK, D, D), "w", CMP_BLOCK * D),
        ("nsa_qn_g", (D,), "g", 1),
        ("nsa_kn_g", (3, D), "g", 1),
        ("w_out", (MIX_WIDTH, D_MODEL), "w", MIX_WIDTH),
        ("norm2_g", (D_MODEL,), "g", 1),
        ("mem_norm_g", (D_MODEL,), "g", 1),
        ("w_xq", (D_MODEL, XATTN_HEADS * XATTN_HEAD_DIM), "w", D_MODEL),
        ("w_xk", (D_MODEL, XATTN_HEADS * XATTN_HEAD_DIM), "w", D_MODEL),
        ("w_xv", (D_MODEL, XATTN_HEADS * XATTN_HEAD_DIM), "w", D_MODEL),
        ("xq_norm_g", (XATTN_HEAD_DIM,), "g", 1),
        ("xk_norm_g", (XATTN_HEAD_DIM,), "g", 1),
        ("w_xo", (XATTN_HEADS * XATTN_HEAD_DIM, D_MODEL), "w", XATTN_HEADS * XATTN_HEAD_DIM),
        ("norm3_g", (D_MODEL,), "g", 1),
        ("w_ff_in", (D_MODEL, D_FF), "w", D_MODEL),
        ("w_ff_out", (D_FF, D_MODEL), "w", D_FF),
    ]
    keys = jax.random.split(key, len(specs) + 2)
    out = {
        "x": jax.random.normal(keys[0], (BATCH, SEQ, D_MODEL), jnp.float32),
        "mem": jax.random.normal(keys[1], (BATCH, MEM_LEN, D_MODEL), jnp.float32),
    }
    for k, (name, shape, kind, fan) in zip(keys[2:], specs):
        z = jax.random.normal(k, (DEPTH,) + shape, jnp.float32)
        if kind == "w":
            out[name] = z * (fan ** -0.5)
        elif kind == "g":
            out[name] = 1.0 + 0.02 * z
        else:
            out[name] = 0.02 * z
    return out

def second_block(x, mem, norm1_g, w_in, dsa_cq_g, dsa_ckv_g, w_dsa_uq, w_dsa_ukv, w_idx_q, idx_k_ln_g, idx_k_ln_b,
              dsa_qn_g, dsa_kn_g, nsa_cmp_pe, w_nsa_cmp, nsa_qn_g, nsa_kn_g, w_out, norm2_g, mem_norm_g,
              w_xq, w_xk, w_xv, xq_norm_g, xk_norm_g, w_xo, norm3_g, w_ff_in, w_ff_out):
    for l in range(DEPTH):
        x = x + _hybrid_mixer(_rms_norm(x, norm1_g[l]), w_in[l], dsa_cq_g[l], dsa_ckv_g[l], w_dsa_uq[l],
                              w_dsa_ukv[l], w_idx_q[l], idx_k_ln_g[l], idx_k_ln_b[l], dsa_qn_g[l], dsa_kn_g[l],
                              nsa_cmp_pe[l], w_nsa_cmp[l], nsa_qn_g[l], nsa_kn_g[l], w_out[l])
        x = x + _memory_xattn(_rms_norm(x, norm2_g[l]), mem, mem_norm_g[l], w_xq[l], w_xk[l], w_xv[l],
                              xq_norm_g[l], xk_norm_g[l], w_xo[l])
        x = x + _sq_relu_mlp(_rms_norm(x, norm3_g[l]), w_ff_in[l], w_ff_out[l])
    return x


def setup_inputs(seed=0):
    out = dict(first_inputs(seed))
    for name, value in second_inputs(seed + 1).items():
        if name != "x":
            out[name + "_2"] = value
    return out


def reference(
    x, c, ctx, c_ctx, w_ada, b_ada, norm_mix, norm_ffn, w_in, gla_lr_w, gla_lr_b, gla_norm,
    w_branch_gla, w_branch_ret, w_out, w_router_group, b_router_group, w_router_expert,
    b_router_expert, w_expert_gate, w_expert_up, w_expert_down, norm_final, mem_2, norm1_g_2,
    w_in_2, dsa_cq_g_2, dsa_ckv_g_2, w_dsa_uq_2, w_dsa_ukv_2, w_idx_q_2, idx_k_ln_g_2,
    idx_k_ln_b_2, dsa_qn_g_2, dsa_kn_g_2, nsa_cmp_pe_2, w_nsa_cmp_2, nsa_qn_g_2, nsa_kn_g_2,
    w_out_2, norm2_g_2, mem_norm_g_2, w_xq_2, w_xk_2, w_xv_2, xq_norm_g_2, xk_norm_g_2, w_xo_2,
    norm3_g_2, w_ff_in_2, w_ff_out_2,
):
    x = first_block(
        x, c, ctx, c_ctx, w_ada, b_ada, norm_mix, norm_ffn, w_in, gla_lr_w, gla_lr_b, gla_norm,
        w_branch_gla, w_branch_ret, w_out, w_router_group, b_router_group, w_router_expert,
        b_router_expert, w_expert_gate, w_expert_up, w_expert_down, norm_final,
    )
    return second_block(
        x, mem_2, norm1_g_2, w_in_2, dsa_cq_g_2, dsa_ckv_g_2, w_dsa_uq_2, w_dsa_ukv_2,
        w_idx_q_2, idx_k_ln_g_2, idx_k_ln_b_2, dsa_qn_g_2, dsa_kn_g_2, nsa_cmp_pe_2,
        w_nsa_cmp_2, nsa_qn_g_2, nsa_kn_g_2, w_out_2, norm2_g_2, mem_norm_g_2, w_xq_2, w_xk_2,
        w_xv_2, xq_norm_g_2, xk_norm_g_2, w_xo_2, norm3_g_2, w_ff_in_2, w_ff_out_2,
    )


_drawn_inputs = setup_inputs


def setup_inputs(seed=0):
    import zlib

    import numpy as np

    out = dict(_drawn_inputs(seed))
    spreads = {}
    factors = {'b_router_group': 8.0,
     'b_router_expert': 2.759,
     'norm1_g_2': 2.772,
     'dsa_cq_g_2': 3.261,
     'dsa_ckv_g_2': 8.0,
     'idx_k_ln_g_2': 3.867,
     'idx_k_ln_b_2': 4.706,
     'dsa_qn_g_2': 8.0,
     'dsa_kn_g_2': 8.0,
     'nsa_cmp_pe_2': 8.0,
     'nsa_qn_g_2': 8.0,
     'nsa_kn_g_2': 8.0,
     'norm2_g_2': 8.0,
     'mem_norm_g_2': 8.0,
     'xq_norm_g_2': 8.0,
     'xk_norm_g_2': 8.0,
     'norm3_g_2': 9.602}
    for name, (base, spread) in spreads.items():
        noise = np.random.default_rng([zlib.crc32(name.encode()), seed]).standard_normal(out[name].shape)
        drawn = base * np.exp(spread * noise) if base else spread * noise
        out[name] = __import__('jax').numpy.asarray(drawn.astype(out[name].dtype))
    for name, factor in factors.items():
        out[name] = (out[name] * factor).astype(out[name].dtype)
    return out
```

```python
import numpy as np
import concourse.bass as bass
from concourse import mybir
from contextlib import ExitStack

F32 = mybir.dt.float32
U32 = mybir.dt.uint32
ALU = mybir.AluOpType
ACT = mybir.ActivationFunctionType
AX = mybir.AxisListType

P = 128
L = 256
NT = L // P
D = 1024
KD = D // P
HEADS, DK, DV = 4, 128, 256
RANK = 16
TAU = 16.0
EPS = 1e-6
GROUPS, PER_GROUP = 4, 8
EXPERTS, FF = 32, 256
PAIRS = EXPERTS // 2
CAP = 64
BIG = 1e30

HD = 64
H2 = 8
TOPK = 64
NCMP = 15
IDX_SCALE = 8 ** -0.5 * 64 ** -0.5
KV0 = 968
XH, XD = 4, 128
FF2 = 4096

TW = 2048
TC = TW // KD
RING = 6
NB = 4


def const_layout():
    sizes = [("ident", P), ("perm", P), ("upper", P), ("ones", P), ("lower", P), ("after", P),
             ("before", P), ("decay", HEADS * 2 * L), ("qdec", 2 * HEADS * L), ("kdec", 16),
             ("cosf", L), ("sinf", L), ("cos2", 64), ("sin2", 64), ("cosc", 32), ("sinc", 32),
             ("causal", 384), ("cmask", 30), ("tie4", 4), ("tie32", 32), ("slots", 64)]
    at, where = 0, {}
    for name, n in sizes:
        where[name] = (at, n)
        at += n
    return where, at


def constants():
    where, n = const_layout()
    c = np.zeros((P, n), np.float32)

    def put(name, a):
        at, m = where[name]
        c[:a.shape[0], at:at + m] = a.reshape(a.shape[0], m)

    i = np.arange(P)
    put("ident", np.eye(P))
    partner = (i // 64) * 64 + (i % 64 + 32) % 64
    perm = np.zeros((P, P))
    perm[partner, i] = 1
    put("perm", perm)
    put("upper", (i[:, None] <= i[None, :]) * 1.0)
    put("ones", np.ones((P, P)))
    put("lower", (i[:, None] >= i[None, :]) * 1.0)
    put("after", (i[:, None] > i[None, :]) * 1.0)
    put("before", (i[:, None] < i[None, :]) * 1.0)
    h = np.arange(HEADS)
    lgf, lgb = np.log1p(-np.exp2(-5.0 - h)), np.log1p(-np.exp2(-5.5 - h))
    s = np.arange(L).reshape(NT, P)
    t = np.arange(L)
    rel = t[None, None, :] - s.T[:, :, None]
    decay = np.stack([np.where(rel >= 0, np.exp(np.abs(rel) * lgf[k]), np.exp(np.abs(rel) * lgb[k]))
                      for k in h], 1) * DK ** -0.5
    put("decay", decay)
    qdec = np.stack([np.exp((t + 1.0) * lgf[:, None]), np.exp((L - t) * lgb[:, None])])
    put("qdec", np.broadcast_to(qdec[None], (P, 2, HEADS, L)))
    kdec = np.stack([np.exp((L - 1.0 - s.T)[:, :, None] * lgf), np.exp(s.T[:, :, None] * lgb)], 1) * DK ** -0.5
    put("kdec", kdec)
    inv = (10000.0 ** (-np.arange(32, dtype=np.float32) / 32)).astype(np.float32)
    rows, cols = np.repeat(np.arange(L // 64), 64), np.tile(np.arange(64), L // 64)
    ang = np.concatenate([inv[:, None] * rows, inv[:, None] * rows, inv[:, None] * cols, inv[:, None] * cols])
    sign = np.where(i % 64 < 32, -1.0, 1.0)[:, None]
    put("cosf", np.cos(ang))
    put("sinf", np.sin(ang) * sign)
    ang2 = s.T[:, :, None] * inv
    put("cos2", np.cos(ang2))
    put("sin2", np.sin(ang2))
    end = np.arange(15) * 16 + 31
    put("cosc", np.cos(end[:, None] * inv))
    put("sinc", np.sin(end[:, None] * inv))
    tri = np.where(i[None, :] <= i[:, None], 0.0, -BIG)
    put("causal", np.concatenate([tri, np.zeros((P, P)), tri], 1))
    put("cmask", np.where(end <= s.T[:, :, None], 0.0, -BIG))
    put("tie4", np.broadcast_to(4.0 - np.arange(4), (P, 4)))
    put("slots", np.broadcast_to(np.arange(64), (P, 64)))
    put("tie32", np.broadcast_to(32.0 - np.arange(32), (P, 32)))
    return c


class Count:

    def __init__(self):
        self.n = 0

    def one(self):
        self.n += 1
        return self.n


COLS = [("b_sh1", 8), ("b_sc1", 8), ("norm_mix", 8), ("b_sh2", 8), ("b_sc2", 8), ("norm_ffn", 8),
        ("gla_norm", 2), ("norm1", 8), ("norm2", 8), ("mem_norm", 8), ("norm3", 8), ("cq_g", 2),
        ("ckv_g", 1), ("xq_g", 1), ("xk_g", 1), ("pe", 64)]
ROWS = [("router_b", 36), ("dsa_qn", 64), ("nsa_qn", 64), ("dsa_kn", 64), ("kn_slc", 64),
        ("kn_win", 64), ("idx_g", 64), ("idx_b", 64), ("kn_cmp", 64)]


def offsets(table):
    at, where = 0, {}
    for name, n in table:
        where[name] = (at, n)
        at += n
    return where, at


GATE_TILES = 8


def plan():
    sums, freed = [], []

    def tile(*names):
        sums.extend(names)
        freed.append(("sum", len(sums)))

    sums.extend(f"mt{k}" for k in range(4))
    for j in range(2):
        tile(f"xk{j}")
    for j in range(2):
        tile(f"xv{j}")
    sums.extend(["xkT0", "xkT1"])
    for b in range(2):
        freed.extend([("ada", b + 1)] * 4)
    sums.extend(f"x{k}" for k in range(KD))
    tile("lr")
    sums.extend(f"z{i}{d}" for i in range(4) for d in range(2))
    for j in range(2):
        tile(f"gk{j}", f"gkc{j}")
    for j in range(4):
        tile(f"gv{j}", f"gvc{j}")
    sums.extend(f"e{d}{s}" for d in range(2) for s in range(2))
    for j in range(2):
        tile(f"gq{j}")
    for j in range(2):
        tile(f"rk{j}", f"rkc{j}")
    for j in range(4):
        tile(f"rv{j}", f"rvc{j}")
    for j in range(2):
        tile(f"rq{j}")
    sums.extend(f"sg{h}" for h in range(HEADS))
    sums.extend(f"sr{h}" for h in range(HEADS))
    sums.append("fac0")
    for i in range(8):
        tile(f"gate{i}")
        if i < 7:
            sums.append(f"fac{i + 1}")
        tile(f"m{i}")
    for b in range(4):
        freed.extend([("ada", 2 + b + 1)] * 4)
    sums.extend(["g1a", "g1b", "mod2", "g2a", "g2b"])
    sums.extend(f"ot{k}" for k in range(8))
    for j in range(4):
        tile(f"bg{j}")
        tile(f"br{j}")
    for j in range(4):
        tile(f"wo{j}")
    sums.extend(f"h2{k}" for k in range(4))
    sums.extend(["rt", "rank"])
    moe_at, moe_sums = len(freed), len(sums)
    for i in range(PAIRS):
        freed.extend([("g", i + 1)] * 2 + [("u", i + 1)] * 2 + [("y", 2 * i + 2)] * 2)
    sums.extend(f"p{k}" for k in range(4))
    for j in range(7):
        tile(f"pj{j}")
    sums.extend(["kb", "cT0", "cT1"])
    tile("qd0", "qd1", "qi0", "qi1")
    sums.append("kvd")
    tile("ck0", "ck1")
    tile("cv0", "cv1")
    sums.append("kcT")
    sums.extend(f"hT{n}" for n in range(9))
    sums.extend(f"cp{n}" for n in range(4))
    sums.extend(["co0", "co1"])
    sums.extend(f"aT{k}" for k in range(4))
    for j in range(4):
        tile(f"ao{j}")
    sums.extend(f"q2{k}" for k in range(4))
    for j in range(2):
        tile(f"xq{j}")
    sums.extend(["xqT0", "xqT1", "oxT0", "oxT1"])
    for j in range(2):
        tile(f"xp{j}0", f"xp{j}1")
    sums.extend(f"q3{k}" for k in range(4))
    for j in range(16):
        tile(f"ff{j}")
    freed.extend(("ffo", j + 1) for j in range(16))
    return sums, freed, moe_at, moe_sums


SUMS, FREED, MOE_AT, MOE_SUMS = plan()
NO = {name: n for n, name in enumerate(SUMS)}


def program(nc, stream, cdram, coldram, rowdram, biasdram, x, ctxt, cvec, wlr_d, wr_d, mem, wukv_d, out):
    where, nconst = const_layout()
    colat, ncol = offsets(COLS)
    rowat, nrow = offsets(ROWS)
    st = ExitStack()
    with st:
        def sb(name, shape):
            return st.enter_context(nc.sbuf_tensor(name, shape, F32))

        def sem(name):
            return st.enter_context(nc.semaphore(name))

        ring = sb("ring", [P, RING, TW])
        consts = sb("consts", [P, nconst])
        cols = sb("cols", [P, ncol])
        rows = sb("rows", [P, nrow])
        hTl = sb("hTl", [P, KD * L])
        hTc = sb("hTc", [P, KD * L])
        arena = sb("arena", [P, 26624])
        cv = sb("cv", [P, KD * 2])
        sc = sb("sc", [P, KD * 2])
        mod1 = sb("mod1", [P, 32])
        mod2 = sb("mod2", [P, 16])
        wr = sb("wr", [P, KD * 36])
        ss = sb("ss", [P, 4])
        ms = sb("ms", [P, 4])
        rt = sb("rt", [P, 4])
        rs = sb("rs", [P, 4])
        mid = sb("mid", [P, 2 * 12])
        stats = sb("stats", [P, 2 * 6])
        mv = sb("mv", [P, 8 * NT * 2])
        hv = sb("hv", [P, 16])
        hr = sb("hr", [P, 16])
        wukv = sb("wukv", [P, 128])
        memkv = sb("memkv", [P, 2048])
        over_i = st.enter_context(nc.sbuf_tensor("over_i", [P, 1], mybir.dt.int32))
        hms = sb("hms", [P, 64])
        hrt = sb("hrt", [P, 64])
        smx = sb("smx", [P, 4 * 2])
        ssum = sb("ssum", [P, 2 * 8])
        top8 = sb("top8", [P, 16])

        def C(name):
            at, n = where[name]
            return consts[:, at:at + n]

        def col(name, k):
            return cols[:, colat[name][0] + k:colat[name][0] + k + 1]

        def cols_of(name):
            return cols[:, colat[name][0]:colat[name][0] + colat[name][1]]

        def row(name):
            return rows[:, rowat[name][0]:rowat[name][0] + rowat[name][1]]

        def region(at, *dims):
            n = int(np.prod(dims))
            v = arena[:, at:at + n]
            names = "abcd"[:len(dims)]
            if len(dims) == 1:
                return v
            return v.rearrange("p (%s) -> p %s" % (" ".join(names), " ".join(names)),
                               **{names[k]: dims[k] for k in range(1, len(dims))})

        ident, ones = C("ident"), C("ones")
        hl = hTl[:, :].rearrange("p (k t) -> p k t", k=KD)
        hc = hTc[:, :].rearrange("p (k t) -> p k t", k=KD)
        QK, V, ST, FA, LC, LL, CX, SC, GT = 0, 4096, 8192, 12288, 14336, 16384, 18432, 24576, 25600
        xr = region(FA, 4, D)
        junk = region(ST, D)
        ada_rows = region(QK, 2 * TC)
        lrT = region(SC, 512)
        wlr = region(GT, 1024)
        spt = region(FA, 2, 512)
        la = region(LC, 4, 2, HEADS * DK)
        gq, gk = region(QK, HEADS, L), region(QK + 1024, HEADS, L)
        rqk = region(QK + 2048, HEADS, 2, L)
        gv, rv = region(V, NT, HEADS * DV), region(V + 2048, NT, HEADS * DV)
        sg, sr = region(ST, HEADS, 2, DV), region(ST + 2048, HEADS, 2, DV)
        kd_g, kd_r = region(FA, 2, NT, 512), region(LC, 2, NT, 512)
        fac = [region(FA, 2048), region(LC, 2048)]
        gkc, gvc = region(CX, NT, 512), region(CX + 1024, NT, 1024)
        rkc, rvc = region(CX + 3072, NT, 512), region(CX + 4096, NT, 1024)
        mT = region(CX, 16, L)
        og = [hTc[:, :].rearrange("p (h v) -> p h v", h=8), region(CX + 4096, 8, DV)]
        scT = [region(SC, 512), region(SC + 512, 512)]
        gate = [region(GT, NT, DV), region(GT + 512, NT, DV)]
        oT = region(QK, 16, L)
        g1bc, g2bc = region(V, D), region(V + 1024, D)
        ada2 = region(V + 2048, 4 * TC)
        tmp = [region(V + 3072, 512), region(V + 3584, 512)]
        yT = region(ST, KD, L)
        hlat = region(ST + 2048, NT, D)
        xn2 = region(QK, NT, D)
        rout = QK + 2048
        h2T = region(FA, KD, L)
        Pm, Pw = region(LC, NT, 2 * CAP), region(LC + 256, NT, 2 * CAP)
        sil, hid = region(LC + 512, FF), region(LC + 768, FF)
        hT_PT = region(LC + 1024, 512)
        xgs = region(LC + 1536, KD, 2 * CAP)
        ysb = region(LC + 2560, D)
        pos, cw = region(LC + 3584, NT, 36), region(LC + 3712, NT, 36)
        rank = region(LC + 3840, 3, 64)
        lg = region(rout, NT, 36)
        ge = region(rout + 80, NT, 4)
        sel = region(rout + 88, NT, 4)
        e1 = region(rout + 96, NT, 32)
        oh1 = region(rout + 160, NT, 32)
        oh2 = region(rout + 224, NT, 32)
        oh = region(rout + 288, NT, 32)
        r2 = [region(rout + 352 + 2 * k, NT) for k in range(12)]

        memx = hTc[:, :].rearrange("p (i d) -> p i d", i=NT)
        mT2 = hl
        kxT = memkv[:, 0:1024].rearrange("p (h t) -> p h t", h=XH)
        vx = memkv[:, 1024:2048].rearrange("p (i d) -> p i d", i=NT)
        kx = region(V, NT, 512)
        ksq = region(V + 1024, NT * XH, XD)
        h1T = region(FA, KD, L)
        PC = 1792
        p2 = region(LC, NT, PC)
        R = region(17920, NT, 36, HD)
        R2 = region(0, NT, 36, HD)
        RT = region(17920, 18, L)
        cq = region(4608, NT, 384)
        cT = region(5376, 3, L)
        kbT = region(6144, 2, L)
        BL = region(6656, 2, 32, NCMP)
        KC, VC = region(7616, 2, HD), region(7744, 2, HD)
        KCD = region(7872, 2, 2, HD)
        kcT = region(8128, 2, 16)
        VD = region(8192, NT, HD)
        wsc = region(8320, NT, H2)
        gates = region(8336, NT, H2, 3)
        kr = region(8384, 2, HD)
        tm = [region(8576, 512), region(9088, 512)]
        sqa, sqb = region(22528, NT, 16, HD), region(24576, NT, 5, HD)
        t1, t2 = region(22528, 768), region(23296, 768)
        sS = [region(22528 + 384 * n, 384) for n in range(3)]
        pT = [region(23680 + 384 * n, 384) for n in range(3)]
        iacc, ibias = region(24832, 384), region(25216, 384)
        rel = [region(25600, 384), region(25984, 384)]
        cS = region(9600, 2 * NT * 4 * 16)
        cmx, crs = region(9856, 16), region(9872, 16)
        PCT = region(FA, 16, P)
        OA = region(0, NT, D)
        oT2 = region(2048, KD, L)
        xn3 = region(4608, NT, D)
        hT3 = region(FA, KD, L)
        qx, qxT = region(22528, NT, 512), region(23552, XH, L)
        xP = [region(24576, 512), region(25088, 512)]
        xPT = [region(25600, 512), region(26112, 512)]
        qsq = region(2048, NT * XH, XD)
        ox = region(0, NT, 512)
        oxT = region(1024, XH, L)
        ffh = region(LC, 32, L)

        bank = [st.enter_context(nc.psum_tensor(f"bank{k}", [P, 512], F32)) for k in range(8)]
        X, Y = bank[4], bank[5]
        O = [bank[6], bank[7]]
        acc = bank[4:8]

        tile_loaded = [sem(f"tile_loaded{k}") for k in range(RING)]
        consts_in, x_in, small_in, out_done = sem("consts_in"), sem("x_in"), sem("small_in"), sem("out_done")
        rows_in, reload_in, bias_in, nfin_in = sem("rows_in"), sem("reload_in"), sem("bias_in"), sem("nfin_in")
        sum_ready, sum_taken = sem("sum_ready"), sem("sum_taken")
        ada_ready, rows_ready, adaT_ready, mod_ready = sem("ada_ready"), sem("rows_ready"), sem("adaT_ready"), sem("mod_ready")
        sc_ready = sem("sc_ready")
        squares, means, roots, normed = sem("squares"), sem("means"), sem("roots"), sem("normed")
        lr_ones, rows_zero = sem("lr_ones"), sem("rows_zero")
        la_ready, ctxk_ready = sem("la_ready"), sem("ctxk_ready")
        factors, scores, scores_taken, values, values_taken = (
            sem("factors"), sem("scores"), sem("scores_taken"), sem("values"), sem("values_taken"))
        head_var, head_root, og_ready = sem("head_var"), sem("head_root"), sem("og_ready")
        gbc_ready, mod2_ready, y_done, res_done = sem("gbc_ready"), sem("mod2_ready"), sem("y_done"), sem("res_done")
        rt_sub, rt_exp, rt_dv, rt_ev = sem("rt_sub"), sem("rt_exp"), sem("rt_dv"), sem("rt_ev")
        oh_ready, over_ready, acc_open = sem("oh_ready"), sem("over_ready"), sem("acc_open")

        class Round:

            def __init__(self, tag):
                self.g_done, self.u_done = sem(tag + "gates_done"), sem(tag + "ups_done")
                self.xg_ready, self.xg_taken = sem(tag + "gathered"), sem(tag + "gathered_taken")
                self.t_ready, self.t_taken = sem(tag + "turned"), sem(tag + "turned_taken")
                self.y_ready, self.y_taken = sem(tag + "downs_done"), sem(tag + "downs_taken")
                self.p_ready, self.pw_ready = sem(tag + "places"), sem(tag + "weighted")
                self.sil_ready, self.hid_ready = sem(tag + "silus"), sem(tag + "hidden")
                self.added = sem(tag + "added")

        main, more = Round("moe_"), Round("more_")
        main.ahead, more.ahead = 0, 1
        moved = sem("moved")
        more_loaded = [sem(f"more_loaded{k}") for k in range(RING)]
        moe_done, x2_ready = sem("moe_done"), sem("x2_ready")
        mem_in = sem("mem_in")
        head_ms, head_rt = sem("head_ms"), sem("head_rt")
        heads_ready, cT_ready, bl_ready = sem("heads_ready"), sem("cT_ready"), sem("bl_ready")
        kc_ready, gates_ready = sem("kc_ready"), sem("gates_ready")
        idx_ready, idx_relu, idx_taken = sem("idx_ready"), sem("idx_relu"), sem("idx_taken")
        cs_ready, cs_sub, cs_exp = sem("cs_ready"), sem("cs_sub"), sem("cs_exp")
        s_ready, s_max, probs, pt_ready, pt_taken, av_done = (
            sem("s_ready"), sem("s_max"), sem("probs"), sem("pt_ready"), sem("pt_taken"), sem("av_done"))
        o_read, o_taken, x1_done = sem("o_read"), sem("o_taken"), sem("x1_done")
        kx_ready, qx_ready, ox_ready = sem("kx_ready"), sem("qx_ready"), sem("ox_ready")
        ff_ready, ffo_done, x_final = sem("ff_ready"), sem("ffo_done"), sem("x_final")
        act_step, dve_step = sem("act_step"), sem("dve_step")
        block = st.enter_context(nc.Block())

        @block.sync
        def _(sp):
            def load(t):
                if t >= RING:
                    kind, n = FREED[t - RING]
                    sp.wait_ge({"sum": sum_ready, "ada": ada_ready, "g": main.g_done, "u": main.u_done,
                                "y": main.y_ready, "ffo": ffo_done}[kind], n)
                sp.dma_start(ring[:, t % RING, :], stream[t]).then_inc(tile_loaded[t % RING], 16)

            for t in range(MOE_AT + RING):
                load(t)
            with sp.Fori(1, PAIRS) as i:
                for s in range(RING):
                    if s < 4:
                        sp.wait_ge((main.g_done, main.u_done)[s // 2], i)
                    else:
                        sp.wait_ge(main.y_ready, i * 2)
                    p = (MOE_AT + s) % RING
                    sp.dma_start(ring[:, p, :], stream[i * RING + (MOE_AT + s)]).then_inc(tile_loaded[p], 16)
            sp.wait_ge(over_ready, 1)
            over = sp.value_load(over_i[0:1, 0:1], min_val=0, max_val=1)
            with sp.If(over > 0):
                sp.wait_ge(main.y_ready, 2 * PAIRS)
                with sp.Fori(0, L // CAP - 1) as r:
                    with sp.Fori(0, PAIRS) as i:
                        for s in range(RING):
                            if s < 4:
                                sp.wait_ge((more.g_done, more.u_done)[s // 2], r * PAIRS + (i + 1))
                            else:
                                sp.wait_ge(more.y_ready, r * (2 * PAIRS) + (i * 2 + 2))
                            p = (MOE_AT + s) % RING
                            sp.dma_start(ring[:, p, :], stream[i * RING + (MOE_AT + s)]).then_inc(more_loaded[p], 16)
                sp.wait_ge(more.y_ready, 2 * PAIRS * (L // CAP - 1) + 2)
            for t in range(MOE_AT + 3 * EXPERTS, len(FREED)):
                load(t)
            sp.wait_ge(x_final, 4)
            sp.dma_start(out.rearrange("b (i p) d -> p (b i) d", p=P), hlat).then_inc(out_done, 16)
            sp.wait_ge(out_done, 16)

        @block.gpsimd
        def _(pool):
            pool.dma_start(rows[:, :], rowdram.partition_broadcast(P)).then_inc(rows_in, 16)
            pool.memset(ada_rows, 0.0).then_inc(rows_zero, 1)
            pool.wait_ge(values, 8)
            pool.dma_start(hlat, x.rearrange("b (i p) d -> p (b i) d", p=P)).then_inc(reload_in, 16)
            pool.memset(ada2, 0.0).then_inc(rows_zero, 1)
            pool.dma_start(region(V, 2048), biasdram[0:2048].partition_broadcast(P)).then_inc(bias_in, 16)
            pool.wait_ge(res_done, 4)
            pool.dma_start(g1bc, biasdram[2048:3072].partition_broadcast(P)).then_inc(nfin_in, 16)

        @block.scalar
        def _(act):
            step = Count()
            act.dma_start(cv[:, :], cvec).then_inc(small_in, 16)
            act.dma_start(memx, mem.rearrange("b (i p) d -> p (b i) d", p=P)).then_inc(mem_in, 16)
            act.dma_start(consts[:, :], cdram).then_inc(consts_in, 16)
            act.dma_start(xr[:, 2:4, :], x.rearrange("b (i p) d -> p (b i) d", p=P)).then_inc(x_in, 16)
            act.dma_start(xr[:, 0:2, :], ctxt.rearrange("b (i p) d -> p (b i) d", p=P)).then_inc(x_in, 16)
            act.dma_start(cols[:, :], coldram).then_inc(small_in, 16)
            act.dma_start(wlr[0:33, :], wlr_d).then_inc(small_in, 16)
            act.dma_start(wr[:, :], wr_d).then_inc(small_in, 16)
            act.dma_start(wukv[:, :], wukv_d).then_inc(small_in, 16)
            taken = Count()

            def take(name):
                assert NO[name] == taken.n, (name, SUMS[taken.n])
                act.wait_ge(sum_ready, NO[name] + 1)
                return bank[NO[name] % NB]

            def copy(name, dst, func=ACT.Copy, scale=1.0, two=256):
                b = take(name)
                act.activation(dst, b[:, :].rearrange("p (a b) -> p a b", b=two), func, scale=scale).then_inc(sum_taken, 1)
                taken.one()

            def turn_scaled(name, dst, k, gain):
                b = take(name)
                for n in range(2):
                    act.activation(dst[:, 2 * k + n, :], b[:, 256 * n:256 * n + 256], ACT.Copy,
                                   scale=col(gain, 2 * k + n)).then_inc((act_step, sum_taken)[n], 1)
                step.one()
                taken.one()

            act.wait_ge(small_in, 16 * 5)
            act.activation(sc[:, :], cv[:, :], ACT.Silu).then_inc(sc_ready, 1)
            sq = Count()

            def row_squares(src, n, junk=junk):
                for i in range(n):
                    act.activation(junk, src[:, i, :], ACT.Square, accum_out=ss[:, i:i + 1]).then_inc(squares, 1)
                    act.wait_ge(squares, sq.one())

            act.wait_ge(mem_in, 16)
            row_squares(memx, 2)
            act.wait_ge(means, 1)
            act.activation(rt[:, 0:2], ms[:, 0:2], ACT.Sqrt).then_inc(roots, 1)
            act.wait_ge(x_in, 32)
            act.wait_ge(normed, 2)
            row_squares(xr, 4)
            act.wait_ge(means, 2)
            act.activation(rt[:, 0:4], ms[:, 0:4], ACT.Sqrt).then_inc(roots, 1)
            for k in range(4):
                turn_scaled(f"mt{k}", mT2, k, "mem_norm")
            for j in range(2):
                copy(f"xk{j}", kx[:, :, TC * j:TC * j + TC])
            for j in range(2):
                copy(f"xv{j}", vx[:, :, TC * j:TC * j + TC])
            act.wait_ge(head_ms, 1)
            act.activation(hrt[:, 0:8], hms[:, 0:8], ACT.Sqrt).then_inc(head_rt, 1)
            for k in range(2):
                copy(f"xkT{k}", kxT[:, 2 * k:2 * k + 2, :], scale=col("xk_g", 0))
            act.wait_ge(ada_ready, 2)
            act.wait_ge(rows_zero, 1)
            for g in range(4):
                act.activation(ada_rows[32 * g:32 * g + 2, :], Y[32 * g:32 * g + 2, :], ACT.Copy).then_inc(rows_ready, 1)
            act.wait_ge(mod_ready, 1)
            for k in range(KD):
                b = take(f"x{k}")
                act.activation(hc[:, k, :], b[:, 0:L], ACT.Identity, bias=mod1[:, 2 * k + 1:2 * k + 2],
                               scale=mod1[:, 16 + 2 * k + 1:16 + 2 * k + 2]).then_inc(act_step, 1)
                step.one()
                act.activation(hl[:, k, :], b[:, L:2 * L], ACT.Identity, bias=mod1[:, 2 * k:2 * k + 1],
                               scale=mod1[:, 16 + 2 * k:16 + 2 * k + 1]).then_inc(sum_taken, 1)
                taken.one()

            b = take("lr")
            act.activation(lrT[0:32, :], b[0:32, :], ACT.Copy).then_inc(sum_taken, 1)
            taken.one()
            for n in range(8):
                i, d = divmod(n, 2)
                b = take(f"z{i}{d}")
                if n >= 2:
                    act.wait_ge(la_ready, n - 1)
                act.activation(spt[:, n % 2, :], b[:, :], ACT.Abs).then_inc(act_step, 1)
                act.wait_ge(act_step, step.one())
                act.activation(la[:, i, d, :], b[:, :], ACT.Relu, scale=-1.0).then_inc(sum_taken, 1)
                taken.one()
                act.activation(spt[:, n % 2, :], spt[:, n % 2, :], ACT.Exp, scale=-1.0).then_inc(act_step, 1)
                act.wait_ge(act_step, step.one())
                act.activation(spt[:, n % 2, :], spt[:, n % 2, :], ACT.Ln, bias=1.0).then_inc(act_step, 1)
                step.one()
            for j in range(2):
                copy(f"gk{j}", gk[:, 2 * j:2 * j + 2, :])
                copy(f"gkc{j}", gkc[:, :, TC * j:TC * j + TC])
            for j in range(4):
                copy(f"gv{j}", gv[:, :, TC * j:TC * j + TC])
                copy(f"gvc{j}", gvc[:, :, TC * j:TC * j + TC])
            act.wait_ge(la_ready, 8)
            for d in range(2):
                for s in range(2):
                    b = take(f"e{d}{s}")
                    act.activation(kd_g[:, d, s, :], b[:, :], ACT.Exp, scale=-1.0 / TAU).then_inc(sum_taken, 1)
                    taken.one()
            for j in range(2):
                copy(f"gq{j}", gq[:, 2 * j:2 * j + 2, :], scale=DK ** -0.5)
            for j in range(2):
                copy(f"rk{j}", rqk[:, 2 * j:2 * j + 2, 1, :])
                copy(f"rkc{j}", rkc[:, :, TC * j:TC * j + TC])
            for j in range(4):
                copy(f"rv{j}", rv[:, :, TC * j:TC * j + TC])
                copy(f"rvc{j}", rvc[:, :, TC * j:TC * j + TC])
            for j in range(2):
                copy(f"rq{j}", rqk[:, 2 * j:2 * j + 2, 0, :])
            for h in range(HEADS):
                copy(f"sg{h}", sg[:, h, :, :])
            for h in range(HEADS):
                copy(f"sr{h}", sr[:, h, :, :])

            def decays(h):
                b = take(f"fac{h}")
                B = b[:, :].rearrange("p (d t) -> p d t", d=2)
                f = fac[h % 2].rearrange("p (d s) -> p d s", d=2)
                m = mid[:, 12 * (h % 2):12 * (h % 2) + 12].rearrange("p (n d c) -> p n d c", n=2, c=3)
                if h >= 2:
                    act.wait_ge(values, h - 1)
                act.activation(m[:, 0, :, 0:2], B[:, :, 63:256:128], ACT.Copy, scale=1.0 / TAU).then_inc(act_step, 1)
                step.one()
                act.activation(m[:, 0, 0, 2:3], B[:, 0, 127:128], ACT.Copy, scale=1.0 / TAU).then_inc(act_step, 1)
                step.one()
                act.activation(m[:, 0, 1, 2:3], B[:, 1, 128:129], ACT.Copy, scale=1.0 / TAU).then_inc(act_step, 1)
                act.wait_ge(act_step, step.one())
                act.activation(m[:, 1, :, :], m[:, 0, :, :], ACT.Copy, scale=-1.0).then_inc(act_step, 1)
                act.wait_ge(act_step, step.one())
                for d in range(2):
                    for i in range(2):
                        act.activation(f[:, d, 128 * i:128 * i + 128], B[:, d, 128 * i:128 * i + 128], ACT.Exp,
                                       scale=-1.0 / TAU, bias=m[:, 0, d, i:i + 1]).then_inc(act_step, 1)
                        step.one()
                        act.activation(f[:, d, 256 + 128 * i:384 + 128 * i], B[:, d, 128 * i:128 * i + 128], ACT.Exp,
                                       scale=1.0 / TAU, bias=m[:, 1, d, i:i + 1]).then_inc(act_step, 1)
                        step.one()
                    act.activation(f[:, d, 512:768], B[:, d, :], ACT.Exp, scale=-1.0 / TAU).then_inc(act_step, 1)
                    step.one()
                    far, near = (128, 0) if d == 0 else (0, 128)
                    act.activation(f[:, d, 768:896], B[:, d, far:far + 128], ACT.Exp,
                                   scale=-1.0 / TAU, bias=m[:, 0, d, 2:3]).then_inc(act_step, 1)
                    step.one()
                    last = act.activation(f[:, d, 896:1024], B[:, d, near:near + 128], ACT.Exp,
                                          scale=1.0 / TAU, bias=m[:, 1, d, 2:3])
                    if d == 0:
                        last.then_inc(act_step, 1)
                        step.one()
                    else:
                        last.then_inc(sum_taken, 1)
                        taken.one()

            def turned(i):
                act.wait_ge(values, i - 1)
                copy(f"fac{i}", fac[i % 2][:, 0:512].rearrange("p (a b) -> p a b", a=2))

            decays(0)
            for i in range(8):
                if i >= 2:
                    act.wait_ge(values_taken, i - 1)
                copy(f"gate{i}", gate[i % 2], func=ACT.Silu)
                if i + 1 < 4:
                    decays(i + 1)
                elif i < 7:
                    turned(i + 1)
                copy(f"m{i}", mT[:, 2 * i:2 * i + 2, :], func=ACT.Sigmoid)
            act.wait_ge(head_var, 1)
            act.activation(hr[:, :], hv[:, :], ACT.Sqrt).then_inc(head_root, 1)
            act.wait_ge(rows_zero, 2)
            for b2 in range(2):
                act.wait_ge(ada_ready, 2 + 2 * b2 + 2)
                for g in range(4):
                    act.activation(ada2[32 * g:32 * g + 1, 512 * b2:512 * b2 + 512],
                                   bank[4 + b2][32 * g:32 * g + 1, :], ACT.Copy).then_inc(rows_ready, 1)
            gbc_used = 0
            for name in ("g1a", "g1b", "mod2", "g2a", "g2b"):
                b = take(name)
                if name == "mod2":
                    src = b[:, :].rearrange("p (s n g r) -> p s g n r", s=2, n=2, g=4)[:, :, :, :, 0]
                    dst = mod2[:, :].rearrange("p (s g n) -> p s g n", s=2, g=4)
                    for q in range(2):
                        act.activation(dst[:, q, :, :], src[:, q, :, :], ACT.Copy).then_inc((act_step, sum_taken)[q], 1)
                    step.one()
                    taken.one()
                    continue
                if gbc_used >= 2:
                    act.wait_ge(gbc_ready, gbc_used - 1)
                act.activation(tmp[gbc_used % 2], b[:, :], ACT.Copy).then_inc(sum_taken, 1)
                taken.one()
                gbc_used += 1
            for k in range(8):
                if k < 4:
                    b = take(f"ot{k}")
                    act.activation(oT[:, 2 * k, :], b[:, 0:256], ACT.Copy, scale=col("gla_norm", 0)).then_inc(act_step, 1)
                    step.one()
                    act.activation(oT[:, 2 * k + 1, :], b[:, 256:512], ACT.Copy, scale=col("gla_norm", 1)).then_inc(sum_taken, 1)
                    taken.one()
                else:
                    copy(f"ot{k}", oT[:, 2 * k:2 * k + 2, :])
            act.wait_ge(gbc_ready, 4)
            n = 0
            for j in range(4):
                for br in ("bg", "br"):
                    if n >= 2:
                        act.wait_ge(y_done, n - 1)
                    copy(f"{br}{j}", tmp[n % 2].rearrange("p (a b) -> p a b", a=2))
                    n += 1
            for j in range(4):
                if j < 2:
                    act.wait_ge(y_done, 7 + j)
                else:
                    act.wait_ge(res_done, j - 1)
                copy(f"wo{j}", tmp[n % 2].rearrange("p (a b) -> p a b", a=2))
                n += 1
            act.wait_ge(res_done, 4)
            row_squares(hlat, 2)
            act.wait_ge(means, 3)
            act.activation(rt[:, 0:2], ms[:, 0:2], ACT.Sqrt).then_inc(roots, 1)
            act.wait_ge(mod2_ready, 1)
            for k in range(4):
                b = take(f"h2{k}")
                act.activation(h2T[:, 2 * k, :], b[:, 0:256], ACT.Identity, bias=mod2[:, 2 * k:2 * k + 1],
                               scale=mod2[:, 8 + 2 * k:9 + 2 * k]).then_inc(act_step, 1)
                step.one()
                act.activation(h2T[:, 2 * k + 1, :], b[:, 256:512], ACT.Identity, bias=mod2[:, 2 * k + 1:2 * k + 2],
                               scale=mod2[:, 9 + 2 * k:10 + 2 * k]).then_inc(sum_taken, 1)
                taken.one()
            b = take("rt")
            act.activation(lg, b[:, 0:128].rearrange("p (a b) -> p a b", a=2)[:, :, 0:36], ACT.Copy).then_inc(sum_taken, 1)
            taken.one()
            act.wait_ge(rt_sub, 1)
            act.activation(ge, ge, ACT.Exp).then_inc(rt_exp, 1)
            act.wait_ge(rt_dv, 1)
            act.activation(r2[6], r2[5], ACT.Exp).then_inc(rt_ev, 1)
            b = take("rank")
            act.activation(rank, b[:, 0:192].rearrange("p (a b) -> p a b", a=3), ACT.Copy).then_inc(sum_taken, 1)
            taken.one()
            assert taken.n == MOE_SUMS

            def experts(R, r):
                def gathered(half, n):
                    act.wait_ge(R.xg_ready, n)
                    for q in range(4):
                        k = 4 * half + q
                        ins = act.activation(xgs[:, k, :], bank[1 + half][:, 128 * q:128 * q + 128], ACT.Identity,
                                             bias=mod2[:, k:k + 1], scale=mod2[:, 8 + k:9 + k])
                        if q == 3:
                            ins.then_inc(R.xg_taken, 1)

                gathered(0, r * (2 * PAIRS + 2) + 1)
                gathered(1, r * (2 * PAIRS + 2) + 2)
                with act.Fori(0, PAIRS) as i:
                    act.wait_ge(R.u_done, r * PAIRS + (i + (1 + R.ahead)))
                    act.wait_ge(R.hid_ready, r * (PAIRS + 1) + (i + 1))
                    act.activation(sil, bank[0][:, 0:FF], ACT.Silu).then_inc(R.sil_ready, 1)
                    gathered(0, r * (2 * PAIRS + 2) + (i * 2 + 3))
                    act.wait_ge(R.t_ready, r * PAIRS + (i + 1))
                    act.activation(hT_PT, bank[3][:, :], ACT.Copy).then_inc(R.t_taken, 1)
                    gathered(1, r * (2 * PAIRS + 2) + (i * 2 + 4))

            experts(main, 0)
            act.wait_ge(over_ready, 1)
            over = act.value_load(over_i[0:1, 0:1], min_val=0, max_val=1)
            with act.If(over > 0):
                with act.Fori(0, L // CAP - 1) as r:
                    experts(more, r)
            act.wait_ge(moe_done, 4)
            row_squares(hlat, 2)
            act.wait_ge(means, 4)
            act.activation(rt[:, 0:2], ms[:, 0:2], ACT.Sqrt).then_inc(roots, 1)
            act.wait_ge(x2_ready, 2)
            row_squares(hlat, 2)
            act.wait_ge(means, 5)
            act.activation(rt[:, 0:2], ms[:, 0:2], ACT.Sqrt).then_inc(roots, 1)
            for k in range(4):
                turn_scaled(f"p{k}", h1T, k, "norm1")
            for j in range(7):
                copy(f"pj{j}", p2[:, :, TC * j:TC * j + TC])
            act.wait_ge(sum_taken, taken.n)
            act.activation(gates, p2[:, :, 1736:1760].rearrange("p i (h c) -> p i h c", c=3), ACT.Sigmoid).then_inc(gates_ready, 1)
            copy("kb", kbT)
            act.wait_ge(head_ms, 2)
            act.activation(hrt[:, 0:4], hms[:, 0:4], ACT.Sqrt).then_inc(head_rt, 1)
            b = take("cT0")
            for n in range(2):
                act.activation(cT[:, n, :], b[:, 256 * n:256 * n + 256], ACT.Copy,
                               scale=col("cq_g", n)).then_inc((act_step, sum_taken)[n], 1)
            step.one()
            taken.one()
            b = take("cT1")
            act.activation(cT[:, 2, :], b[:, 0:256], ACT.Copy, scale=col("ckv_g", 0)).then_inc(sum_taken, 1)
            taken.one()
            for name, at in (("qd", 0), ("qi", 16)):
                for j in range(NT):
                    copy(f"{name}{j}", R[:, j, at:at + 8, :], two=HD)
            b = take("kvd")
            bv = b[:, 0:256].rearrange("p (i c) -> p i c", i=NT)
            act.activation(R[:, :, 24, :], bv[:, :, 0:HD], ACT.Copy).then_inc(act_step, 1)
            step.one()
            act.activation(VD, bv[:, :, HD:2 * HD], ACT.Copy).then_inc(sum_taken, 1)
            taken.one()
            for kv, dst in (("ck", KC), ("cv", VC)):
                for g in range(2):
                    b = take(f"{kv}{g}")
                    act.activation(dst[0:NCMP, g, :], b[0:NCMP, 0:HD], ACT.Copy).then_inc(sum_taken, 1)
                    taken.one()
            act.wait_ge(head_ms, 3)
            act.activation(hrt[:, 0:44], hms[:, 0:44], ACT.Sqrt).then_inc(head_rt, 1)
            act.wait_ge(head_ms, 4)
            act.activation(hrt[0:NCMP, 44:46], hms[0:NCMP, 44:46], ACT.Sqrt).then_inc(head_rt, 1)
            b = take("kcT")
            act.activation(kcT[:, :, 0:NCMP], b[:, 0:32].rearrange("p (g n) -> p g n", g=2)[:, :, 0:NCMP],
                           ACT.Copy).then_inc(sum_taken, 1)
            taken.one()
            for n in range(9):
                copy(f"hT{n}", RT[:, 2 * n:2 * n + 2, :])
            for h in range(H2):
                act.wait_ge(idx_ready, h + 1)
                if h >= 2:
                    act.wait_ge(idx_taken, h - 1)
                act.activation(rel[h % 2], bank[4 + h % 2][:, 0:384], ACT.Relu).then_inc(idx_relu, 1)
            act.wait_ge(cs_sub, 1)
            act.activation(cS, cS, ACT.Exp).then_inc(cs_exp, 1)
            for n in range(4):
                b = take(f"cp{n}")
                act.activation(PCT[0:NCMP, 4 * n:4 * n + 4, :], b[0:NCMP, :].rearrange("p (a b) -> p a b", a=4),
                               ACT.Copy).then_inc(sum_taken, 1)
                taken.one()
            for j in range(NT):
                b = take(f"co{j}")
                act.activation(tm[j], b[:, :], ACT.Copy).then_inc(sum_taken, 1)
                taken.one()
            for n in range(3 * H2 + 2):
                if n < 3 * H2:
                    act.wait_ge(s_max, n + 1)
                    g, hh = divmod(n, 4)
                    if hh == 0 and g >= 2:
                        act.wait_ge(o_taken, g)
                    sm = ssum[:, 8 * (g % 2):8 * (g % 2) + 8].rearrange("p (i h) -> p i h", i=NT)
                    for i, (a, z) in enumerate(((0, 128), (128, 384))):
                        act.activation(sS[n % 3][:, a:z], sS[n % 3][:, a:z], ACT.Exp,
                                       bias=smx[:, 2 * (n % 4) + i:2 * (n % 4) + i + 1],
                                       accum_out=sm[:, i, hh:hh + 1]).then_inc((act_step, probs)[i], 1)
                    step.one()
                m = n - 1
                if 0 <= m < 3 * H2:
                    act.wait_ge(pt_ready, m + 1)
                    if m >= 3:
                        act.wait_ge(av_done, m - 2)
                    act.activation(pT[m % 3], bank[6 + m % 2][:, 0:384], ACT.Copy).then_inc(pt_taken, 1)
                if m >= 4 and m % 4 == 2 or m == 3 * H2:
                    g = (m - 4) // 4 if m < 3 * H2 else 5
                    act.wait_ge(av_done, 4 * g + 4)
                    if g == 0:
                        act.wait_ge(o_taken, 0 + 1)
                    elif g >= 2:
                        act.wait_ge(o_taken, g)
                    act.activation(tm[g % 2], bank[g % 2][:, :], ACT.Copy).then_inc(o_read, 1)
            for k in range(4):
                copy(f"aT{k}", oT2[:, 2 * k:2 * k + 2, :])
            for j in range(4):
                if j < 2:
                    act.wait_ge(o_taken, 6 + j)
                else:
                    act.wait_ge(x1_done, j - 1)
                copy(f"ao{j}", tm[j % 2].rearrange("p (a b) -> p a b", a=2))
            act.wait_ge(x1_done, 4)
            row_squares(hlat, 2)
            act.wait_ge(means, 6)
            act.activation(rt[:, 0:2], ms[:, 0:2], ACT.Sqrt).then_inc(roots, 1)
            for k in range(4):
                turn_scaled(f"q2{k}", hT3, k, "norm2")
            for j in range(2):
                copy(f"xq{j}", qx[:, :, TC * j:TC * j + TC])
            act.wait_ge(head_ms, 5)
            act.activation(hrt[:, 0:8], hms[:, 0:8], ACT.Sqrt).then_inc(head_rt, 1)
            for k in range(2):
                copy(f"xqT{k}", qxT[:, 2 * k:2 * k + 2, :], scale=col("xq_g", 0))
            for n in range(XH + 1):
                if n < XH:
                    act.wait_ge(s_max, 3 * H2 + n + 1)
                    for i in range(NT):
                        act.activation(xP[n % 2][:, 256 * i:256 * i + 256], bank[4 + n % 2][:, 256 * i:256 * i + 256], ACT.Exp,
                                       scale=XD ** -0.5, bias=smx[:, 2 * n + i:2 * n + i + 1],
                                       accum_out=ssum[:, 4 * i + n:4 * i + n + 1]).then_inc((act_step, probs)[i], 1)
                    step.one()
                m = n - 1
                if m >= 0:
                    act.wait_ge(pt_ready, 3 * H2 + m + 1)
                    if m >= 2:
                        act.wait_ge(av_done, 3 * H2 + m - 1)
                    act.activation(xPT[m % 2], bank[6 + m % 2][:, :], ACT.Copy).then_inc(pt_taken, 1)
            for k in range(2):
                act.wait_ge(av_done, 3 * H2 + 2 * k + 2)
                act.activation(tm[k], bank[k][:, :], ACT.Copy).then_inc(o_read, 1)
            for k in range(2):
                copy(f"oxT{k}", oxT[:, 2 * k:2 * k + 2, :])
            act.wait_ge(ox_ready, 2)
            for n in range(4):
                if n >= 2:
                    act.wait_ge(x1_done, 4 + n - 1)
                copy(f"xp{n // 2}{n % 2}", tm[n % 2].rearrange("p (a b) -> p a b", a=2))
            act.wait_ge(x1_done, 8)
            row_squares(hlat, 2)
            act.wait_ge(means, 7)
            act.activation(rt[:, 0:2], ms[:, 0:2], ACT.Sqrt).then_inc(roots, 1)
            for k in range(4):
                turn_scaled(f"q3{k}", hT3, k, "norm3")
            for j in range(16):
                copy(f"ff{j}", ffh[:, 2 * j:2 * j + 2, :], func=ACT.Relu)
            assert taken.n == len(SUMS)

        @block.tensor
        def _(pe):
            t = Count()
            done = Count()

            def tile():
                n = t.n
                pe.wait_ge(tile_loaded[n % RING], 16 * (n // RING + 1))
                t.one()
                return ring[:, n % RING, :].rearrange("p (k n) -> p k n", k=KD)

            def fresh(name):
                n = done.n
                assert NO[name] == n, (name, SUMS[n])
                if n >= NB:
                    pe.wait_ge(sum_taken, n - NB + 1)
                done.one()
                return bank[n % NB]

            def feature_rows(name, w, h):
                b = fresh(name)
                for n in range(2):
                    for k in range(KD):
                        mm = pe.matmul(b[:, 256 * n:256 * n + 256], w[:, k, 128 * n:128 * n + 128], h[:, k, :],
                                       start=(k == 0), stop=(k == KD - 1))
                mm.then_inc(sum_ready, 1)

            def token_rows(name, w, h):
                b = fresh(name)
                for i in range(NT):
                    for k in range(KD):
                        mm = pe.matmul(b[:, 256 * i:256 * i + 256], h[:, k, 128 * i:128 * i + 128], w[:, k, :],
                                       start=(k == 0), stop=(k == KD - 1))
                mm.then_inc(sum_ready, 1)

            def turn(name, src, k):
                b = fresh(name)
                for n in range(2):
                    for j in range(NT):
                        mm = pe.transpose(b[:, 256 * n + 128 * j:256 * n + 128 * j + 128],
                                          src[:, j, 256 * k + 128 * n:256 * k + 128 * n + 128], ident)
                mm.then_inc(sum_ready, 1)

            pe.wait_ge(consts_in, 16)
            pe.wait_ge(normed, 2)
            for k in range(4):
                turn(f"mt{k}", memx, k)
            pe.wait_ge(sum_taken, NO["mt3"] + 1)
            for j in range(2):
                token_rows(f"xk{j}", tile(), mT2)
            for j in range(2):
                token_rows(f"xv{j}", tile(), mT2)
            pe.wait_ge(kx_ready, 1)
            for k in range(2):
                turn(f"xkT{k}", kx, k)
            pe.wait_ge(sc_ready, 1)
            scv = sc[:, :].rearrange("p (k c) -> p k c", c=2)

            def modulation(b2, out_bank, at, m):
                w = [tile() for _ in range(4)]
                for k in range(KD):
                    for g in range(4):
                        mm = pe.matmul(out_bank[32 * g:32 * g + m, at:at + TC], scv[:, k, 0:m], w[g][:, k, :],
                                       start=(k == 0), stop=(k == KD - 1), skip_group_check=True)
                mm.then_inc(ada_ready, 1)

            for b2 in range(2):
                modulation(b2, Y, TC * b2, 2)
            pe.wait_ge(rows_ready, 4)
            for n in range(4):
                mm = pe.transpose(X[:, 128 * n:128 * n + 128], ada_rows[:, 128 * n:128 * n + 128], ident)
            mm.then_inc(adaT_ready, 1)
            pe.wait_ge(normed, 6)
            for k in range(KD):
                b = fresh(f"x{k}")
                for i in range(4):
                    mm = pe.transpose(b[:, 128 * i:128 * i + 128], xr[:, i, 128 * k:128 * k + 128], ident)
                mm.then_inc(sum_ready, 1)
            pe.wait_ge(sum_taken, NO["x7"] + 1)
            w = tile()
            b = fresh("lr")
            for j, h in ((0, hc), (1, hl)):
                for k in range(KD):
                    mm = pe.matmul(b[0:32, 256 * j:256 * j + 256], w[:, k, 0:32], h[:, k, :],
                                   start=(k == 0), stop=(k == KD - 1))
            mm.then_inc(sum_ready, 1)
            pe.wait_ge(lr_ones, 1)
            pe.wait_ge(sum_taken, NO["lr"] + 1)
            for i in range(4):
                for d in range(2):
                    b = fresh(f"z{i}{d}")
                    pe.matmul(b[:, :], lrT[0:33, 128 * i:128 * i + 128], wlr[0:33, 512 * d:512 * d + 512],
                              start=True, stop=True).then_inc(sum_ready, 1)
            for j in range(2):
                w = tile()
                feature_rows(f"gk{j}", w, hl)
                token_rows(f"gkc{j}", w, hc)
            for j in range(4):
                w = tile()
                token_rows(f"gv{j}", w, hl)
                token_rows(f"gvc{j}", w, hc)
            pe.wait_ge(la_ready, 8)
            after, before = C("after"), C("before")
            for d in range(2):
                for s in range(2):
                    b = fresh(f"e{d}{s}")
                    tri = after if d == 0 else before
                    other = 1 - s
                    cross = (d == 0 and s == 0) or (d == 1 and s == 1)
                    mm = pe.matmul(b[:, :], tri, la[:, s, d, :], start=True, stop=not cross)
                    if cross:
                        mm = pe.matmul(b[:, :], ones, la[:, other, d, :], start=False, stop=True)
                    mm.then_inc(sum_ready, 1)
            for j in range(2):
                feature_rows(f"gq{j}", tile(), hl)
            for j in range(2):
                w = tile()
                feature_rows(f"rk{j}", w, hl)
                token_rows(f"rkc{j}", w, hc)
            for j in range(4):
                w = tile()
                token_rows(f"rv{j}", w, hl)
                token_rows(f"rvc{j}", w, hc)
            for j in range(2):
                feature_rows(f"rq{j}", tile(), hl)
            for name, kd, v, n in (("sg", kd_g, gvc, 4), ("sr", kd_r, rvc, 8)):
                pe.wait_ge(ctxk_ready, n)
                for h in range(HEADS):
                    b = fresh(f"{name}{h}")
                    for d in range(2):
                        for s in range(NT):
                            mm = pe.matmul(b[:, 256 * d:256 * d + 256], kd[:, d, s, 128 * h:128 * h + 128],
                                           v[:, s, 256 * h:256 * h + 256], start=(s == 0), stop=(s == NT - 1))
                    mm.then_inc(sum_ready, 1)

            cum = consts[:, where["upper"][0]:where["upper"][0] + 3 * P]

            def before_factors(i):
                b = fresh(f"fac{i}")
                if i < HEADS:
                    c = slice(128 * i, 128 * i + 128)
                    pe.matmul(b[:, 0:256], la[:, 2, 0, c], cum[:, 0:256], start=True, stop=False)
                    pe.matmul(b[:, 128:256], la[:, 3, 0, c], cum[:, 0:128], start=False, stop=True)
                    pe.matmul(b[:, 256:512], la[:, 3, 1, c], cum[:, 128:384], start=True, stop=False)
                    mm = pe.matmul(b[:, 256:384], la[:, 2, 1, c], cum[:, 256:384], start=False, stop=True)
                else:
                    mm = pe.matmul(b[:, :], C("perm"), rqk[:, i - HEADS, :, :], start=True, stop=True)
                mm.then_inc(sum_ready, 1)

            before_factors(0)
            for i in range(8):
                token_rows(f"gate{i}", tile(), hl)
                f = fac[i % 2]
                pe.wait_ge(factors, i + 1)
                if i >= 1:
                    pe.wait_ge(scores_taken, i)
                if i < HEADS:
                    F = f.rearrange("p (d s) -> p d s", d=2)
                    pe.matmul(X[:, 0:128], F[:, 1, 256:384], F[:, 1, 0:128], start=True, stop=True)
                    pe.matmul(X[:, 128:256], F[:, 0, 896:1024], F[:, 0, 768:896], start=True, stop=True)
                    pe.matmul(X[:, 256:384], F[:, 1, 896:1024], F[:, 1, 768:896], start=True, stop=True)
                    pe.matmul(X[:, 384:512], F[:, 1, 384:512], F[:, 1, 128:256], start=True, stop=True)
                    pe.matmul(Y[:, 0:128], F[:, 0, 256:384], F[:, 0, 0:128], start=True, stop=True)
                    mm = pe.matmul(Y[:, 128:256], F[:, 0, 384:512], F[:, 0, 128:256], start=True, stop=True)
                    qs = [F[:, 0, 512:768], F[:, 1, 512:768]]
                    states, v, h = sg, gv, i
                else:
                    for s in range(NT):
                        mm = pe.matmul(X[:, 256 * s:256 * s + 256], f[:, 256 + 128 * s:384 + 128 * s], f[:, 0:256],
                                       start=True, stop=True)
                    qs = [f[:, 512:768], f[:, 768:1024]]
                    states, v, h = sr, rv, i - HEADS
                mm.then_inc(scores, 1)
                if i < 7:
                    before_factors(i + 1)
                feature_rows(f"m{i}", tile(), hl)
                pe.wait_ge(scores_taken, i + 1)
                if i >= 2:
                    pe.wait_ge(values_taken, i - 1)
                for j in range(NT):
                    o = O[i % 2][:, 256 * j:256 * j + 256]
                    c = slice(128 * j, 128 * j + 128)
                    for s in range(NT):
                        pe.matmul(o, scT[i % 2][:, 256 * s + 128 * j:256 * s + 128 * j + 128],
                                  v[:, s, 256 * h:256 * h + 256], start=(s == 0), stop=False)
                    for d in range(2):
                        mm = pe.matmul(o, qs[d][:, c], states[:, h, d, :], start=False, stop=(d == 1))
                mm.then_inc(values, 1)
            for b2 in range(4):
                modulation(b2, bank[4 + b2 // 2], TC * (b2 % 2), 1)
            pe.wait_ge(rows_ready, 4 + 8)
            for name, b2, n0 in (("g1a", 0, 0), ("g1b", 0, 2), ("mod2", None, 0), ("g2a", 3, 0), ("g2b", 3, 2)):
                b = fresh(name)
                if name == "mod2":
                    for blk in range(4):
                        mm = pe.transpose(b[:, 128 * blk:128 * blk + 128], ada2[:, 256 + 128 * blk:384 + 128 * blk], ident)
                else:
                    for n in range(2):
                        g = n0 + n
                        mm = pe.matmul(b[:, 256 * n:256 * n + 256], ident[:, 32 * g:32 * g + 1].to_broadcast([P, P]),
                                       ada2[:, 256 * b2:256 * b2 + 256], start=True, stop=True)
                mm.then_inc(sum_ready, 1)
            pe.wait_ge(og_ready, 16)
            for k in range(8):
                b = fresh(f"ot{k}")
                for n in range(2):
                    for j in range(NT):
                        mm = pe.transpose(b[:, 256 * n + 128 * j:256 * n + 128 * j + 128],
                                          og[j][:, k, 128 * n:128 * n + 128], ident)
                mm.then_inc(sum_ready, 1)
            pe.wait_ge(sum_taken, NO["ot7"] + 1)
            for j in range(4):
                feature_rows(f"bg{j}", tile(), oT[:, 0:8, :])
                feature_rows(f"br{j}", tile(), oT[:, 8:16, :])
            pe.wait_ge(y_done, 8)
            for j in range(4):
                token_rows(f"wo{j}", tile(), yT)
            pe.wait_ge(normed, 8)
            for k in range(4):
                b = fresh(f"h2{k}")
                for n in range(2):
                    for j in range(NT):
                        mm = pe.transpose(b[:, 256 * n + 128 * j:256 * n + 128 * j + 128],
                                          xn2[:, j, 256 * k + 128 * n:256 * k + 128 * n + 128], ident)
                mm.then_inc(sum_ready, 1)
            pe.wait_ge(sum_taken, NO["h23"] + 1)
            b = fresh("rt")
            wrv = wr[:, :].rearrange("p (k n) -> p k n", k=KD)
            for j in range(NT):
                for k in range(KD):
                    mm = pe.matmul(b[:, 64 * j:64 * j + 36], h2T[:, k, 128 * j:128 * j + 128], wrv[:, k, :],
                                   start=(k == 0), stop=(k == KD - 1))
            mm.then_inc(sum_ready, 1)
            pe.wait_ge(oh_ready, 1)
            b = fresh("rank")
            before = C("before")
            pe.matmul(b[:, 0:32], before, oh[:, 0, :], start=True, stop=True)
            pe.matmul(b[:, 64:96], ones, oh[:, 0, :], start=True, stop=False)
            pe.matmul(b[:, 64:96], before, oh[:, 1, :], start=False, stop=True)
            pe.matmul(b[:, 128:160], ones, oh[:, 0, :], start=True, stop=False)
            pe.matmul(b[:, 128:160], ones, oh[:, 1, :], start=False, stop=True)
            pe.matmul(b[:, 32:64], before, ident[:, 0:32], start=True, stop=True)
            pe.matmul(b[:, 96:128], before, ident[:, 0:32], start=True, stop=True)
            pe.matmul(b[:, 160:192], before, ident[:, 0:32], start=True, stop=True).then_inc(sum_ready, 1)
            assert t.n == MOE_AT and done.n == MOE_SUMS
            pe.wait_ge(sum_taken, MOE_SUMS)

            def experts(R, r, loaded, base):
                def gather(half):
                    for q in range(4):
                        for j in range(NT):
                            k = 4 * half + q
                            mm = pe.matmul(bank[1 + half][:, 128 * q:128 * q + 128], xn2[:, j, 128 * k:128 * k + 128],
                                           Pm[:, j, :], start=(j == 0), stop=(j == NT - 1))
                    mm.then_inc(R.xg_ready, 1)

                def scatter():
                    for j in range(NT):
                        for n in range(2):
                            mm = pe.matmul(acc[2 * j + n][:, :], hT_PT[:, 256 + 128 * j:384 + 128 * j],
                                           ysb[:, 512 * n:512 * n + 512], start=False, stop=False, skip_group_check=True)
                    return mm

                pe.wait_ge(R.p_ready, r * (PAIRS + 1) + 1)
                gather(0)
                gather(1)
                with pe.Fori(0, PAIRS) as i:
                    def weights(s):
                        p = (MOE_AT + s) % RING
                        pe.wait_ge(loaded[p], r * (16 * PAIRS) + (i * 16 + base(s)))
                        return ring[:, p, :]

                    pe.wait_ge(R.xg_taken, r * (2 * PAIRS + 2) + (i * 2 + 2))
                    pe.wait_ge(R.hid_ready, r * (PAIRS + 1) + (i + 1))
                    for a, done_a in enumerate((R.g_done, R.u_done)):
                        w = [weights(2 * a + e).rearrange("p (k n) -> p k n", k=KD) for e in range(2)]
                        for k in range(KD):
                            for e in range(2):
                                mm = pe.matmul(bank[0][CAP * e:CAP * e + CAP, FF * a:FF * a + FF],
                                               xgs[:, k, CAP * e:CAP * e + CAP], w[e][:, k, :],
                                               start=(k == 0), stop=(k == KD - 1), skip_group_check=True)
                        mm.then_inc(done_a, 1)
                    pe.wait_ge(R.p_ready, r * (PAIRS + 1) + (i + 2))
                    pe.wait_ge(R.y_taken, r * (2 * PAIRS + 2) + (i * 2 + 2))
                    gather(0)
                    scatter()
                    pe.wait_ge(R.hid_ready, r * (PAIRS + 1) + (i + 2))
                    pe.wait_ge(R.pw_ready, r * PAIRS + (i + 1))
                    for f in range(2):
                        pe.transpose(bank[3][:, 128 * f:128 * f + 128], hid[:, 128 * f:128 * f + 128], ident)
                    for j in range(NT):
                        mm = pe.transpose(bank[3][:, 256 + 128 * j:384 + 128 * j], Pw[:, j, :], ident)
                    mm.then_inc(R.t_ready, 1)
                    gather(1)
                    pe.wait_ge(R.t_taken, r * PAIRS + (i + 1))
                    wd = [weights(4 + e).rearrange("p (k n) -> p k n", k=2) for e in range(2)]
                    for n in range(2):
                        pe.wait_ge(R.xg_taken, r * (2 * PAIRS + 2) + (i * 2 + (3 + n)))
                        for k in range(2):
                            for e in range(2):
                                mm = pe.matmul(bank[1 + n][CAP * e:CAP * e + CAP, :],
                                               hT_PT[:, 128 * k + CAP * e:128 * k + CAP * e + CAP],
                                               wd[e][:, k, 512 * n:512 * n + 512], start=(k == 0), stop=(k == 1),
                                               skip_group_check=True)
                        mm.then_inc(R.y_ready, 1)
                pe.wait_ge(R.y_taken, r * (2 * PAIRS + 2) + (2 * PAIRS + 2))
                scatter().then_inc(R.added, 1)

            pe.wait_ge(acc_open, 1)
            for n in range(4):
                pe.matmul(acc[n][:, :], hT_PT[:, 0:128], consts[:, 0:512], start=True, stop=False, skip_group_check=True)
            experts(main, 0, tile_loaded, lambda s: 16 * ((MOE_AT + s) // RING + 1))
            pe.wait_ge(over_ready, 1)
            over = pe.value_load(over_i[0:1, 0:1], min_val=0, max_val=1)
            with pe.If(over > 0):
                for s_ in (more.g_done, more.u_done, more.y_ready, more.y_ready):
                    pe.matmul(bank[3][0:1, 0:2], ident[:, 0:1], ident[:, 0:2], start=True, stop=True).then_inc(s_, 1)
                with pe.Fori(0, L // CAP - 1) as r:
                    experts(more, r, more_loaded, lambda s: 16)
            t.n += 3 * EXPERTS
            pe.wait_ge(normed, 10)
            for k in range(4):
                turn(f"p{k}", xn2, k)
            pe.wait_ge(sum_taken, NO["p3"] + 1)
            for j in range(7):
                token_rows(f"pj{j}", tile(), h1T)
            pe.wait_ge(sum_taken, NO["pj6"] + 1)
            b = fresh("kb")
            for kv in range(2):
                for j in range(NT):
                    mm = pe.transpose(b[:, 256 * kv + 128 * j:256 * kv + 128 * j + 128],
                                      p2[:, j, KV0 + 128 * kv:KV0 + 128 * kv + 128], ident)
            mm.then_inc(sum_ready, 1)
            pe.wait_ge(cT_ready, 1)
            for name, tiles in (("cT0", (0, 1)), ("cT1", (2,))):
                b = fresh(name)
                for n, f in enumerate(tiles):
                    for j in range(NT):
                        mm = pe.transpose(b[:, 256 * n + 128 * j:256 * n + 128 * j + 128],
                                          cq[:, j, 128 * f:128 * f + 128], ident)
                mm.then_inc(sum_ready, 1)
            pe.wait_ge(sum_taken, NO["cT1"] + 1)
            tile()
            w = ring[:, (t.n - 1) % RING, :].rearrange("p (k n) -> p k n", k=2)
            for q, name in enumerate(("qd", "qi")):
                for j in range(NT):
                    b = fresh(f"{name}{j}")
                    for k in range(2):
                        mm = pe.matmul(b[:, :], cT[:, k, 128 * j:128 * j + 128], w[:, k, 512 * q:512 * q + 512],
                                       start=(k == 0), stop=(k == 1))
                    mm.then_inc(sum_ready, 1)
            b = fresh("kvd")
            for j in range(NT):
                mm = pe.matmul(b[:, 128 * j:128 * j + 128], cT[:, 2, 128 * j:128 * j + 128], wukv[:, :], start=True, stop=True)
            mm.then_inc(sum_ready, 1)
            pe.wait_ge(bl_ready, 4)
            for kv, name in enumerate(("ck", "cv")):
                tile()
                w = ring[:, (t.n - 1) % RING, :].rearrange("p (l e) -> p l e", l=32)
                for g in range(2):
                    b = fresh(f"{name}{g}")
                    r = slice(64 * g, 64 * g + 64)
                    for l in range(32):
                        mm = pe.matmul(b[0:NCMP, 0:HD], BL[r, kv, l, :], w[r, l, :], start=(l == 0), stop=(l == 31))
                    mm.then_inc(sum_ready, 1)
            pe.wait_ge(kc_ready, 1)
            b = fresh("kcT")
            for g in range(2):
                mm = pe.transpose(b[:, 16 * g:16 * g + NCMP], KCD[0:NCMP, g, :, :].rearrange("p a b -> p (a b)"),
                                  ident[0:NCMP, 0:NCMP])
            mm.then_inc(sum_ready, 1)
            pe.wait_ge(heads_ready, 1)
            for n in range(9):
                b = fresh(f"hT{n}")
                for m in range(2):
                    q = 2 * n + m
                    for j in range(NT):
                        mm = pe.transpose(b[:, 256 * m + 128 * j:256 * m + 128 * j + 128],
                                          R2[:, j, 2 * q:2 * q + 2, :].rearrange("p a b -> p (a b)"), ident)
                mm.then_inc(sum_ready, 1)
            pe.wait_ge(sum_taken, NO["hT8"] + 1)

            def causal_scores(b, qpair, kpair, half):
                r = slice(64 * half, 64 * half + 64)
                pe.matmul(b[:, 0:128], RT[r, qpair, 0:128], RT[r, kpair, 0:128], start=True, stop=True)
                return pe.matmul(b[:, 128:384], RT[r, qpair, 128:256], RT[r, kpair, 0:256], start=True, stop=True)

            for h in range(H2):
                if h >= 2:
                    pe.wait_ge(idx_relu, h - 1)
                causal_scores(bank[4 + h % 2], 8 + h // 2, 17, h % 2).then_inc(idx_ready, 1)
            for par in range(2):
                r = slice(64 * par, 64 * par + 64)
                for j in range(NT):
                    for hh in range(4):
                        h = 2 * hh + par
                        at = 64 * j + 16 * hh
                        mm = pe.matmul(bank[6 + par][:, at:at + NCMP], RT[r, 4 + h // 2, 128 * j:128 * j + 128],
                                       kcT[r, h // 4, 0:NCMP], start=True, stop=True)
                mm.then_inc(cs_ready, 1)
            pe.wait_ge(cs_exp, 1)
            cS5 = cS.rearrange("p (a i h n) -> p a i h n", a=2, i=NT, h=4)
            for n in range(4):
                b = fresh(f"cp{n}")
                for m in range(4):
                    j, h = divmod(4 * n + m, H2)
                    mm = pe.transpose(b[0:NCMP, 128 * m:128 * m + 128], cS5[:, h % 2, j, h // 2, 0:NCMP], ident)
                mm.then_inc(sum_ready, 1)
            pe.wait_ge(sum_taken, NO["cp3"] + 1)
            for j in range(NT):
                b = fresh(f"co{j}")
                for h in range(H2):
                    mm = pe.matmul(b[:, HD * h:HD * h + HD], PCT[0:NCMP, H2 * j + h, :], VC[0:NCMP, h // 4, :],
                                   start=True, stop=True)
                mm.then_inc(sum_ready, 1)

            def head(n):
                kind, h = divmod(n, H2)
                if kind < 2:
                    g = h // 4
                    at = KV0 + 256 * (kind + 1) + 128 + HD * g
                    return 4 + h // 2, 13 + 2 * kind + g, h % 2, lambda k: p2[:, k, at:at + HD]
                return h // 2, 12, h % 2, lambda k: VD[:, k, :]

            pe.wait_ge(sum_taken, NO["co1"] + 1)
            for n in range(3 * H2 + 2):
                if n < 3 * H2:
                    q, k, half, _ = head(n)
                    if n >= 2:
                        pe.wait_ge(s_max, n - 1)
                    else:
                        pe.wait_ge(idx_relu, H2)
                    causal_scores(bank[4 + n % 2], q, k, half).then_inc(s_ready, 1)
                m = n - 1
                if 0 <= m < 3 * H2:
                    pe.wait_ge(probs, m + 1)
                    if m >= 2:
                        pe.wait_ge(pt_taken, m - 1)
                    for c in range(3):
                        mm = pe.transpose(bank[6 + m % 2][:, 128 * c:128 * c + 128], sS[m % 3][:, 128 * c:128 * c + 128], ident)
                    mm.then_inc(pt_ready, 1)
                m = n - 2
                if m >= 0:
                    g, hh = divmod(m, 4)
                    b = bank[g % 2]
                    if hh == 0 and g >= 2:
                        pe.wait_ge(o_read, g - 1)
                    v = head(m)[3]
                    pe.wait_ge(pt_taken, m + 1)
                    T = pT[m % 3]
                    mm = pe.matmul(b[:, HD * hh:HD * hh + HD], T[:, 0:128], v(0), start=True, stop=True)
                    pe.matmul(b[:, 256 + HD * hh:256 + HD * hh + HD], T[:, 128:256], v(0), start=True, stop=False)
                    mm = pe.matmul(b[:, 256 + HD * hh:256 + HD * hh + HD], T[:, 256:384], v(1), start=False, stop=True)
                    mm.then_inc(av_done, 1)
            pe.wait_ge(o_taken, 7)
            for k in range(4):
                turn(f"aT{k}", OA, k)
            pe.wait_ge(sum_taken, NO["aT3"] + 1)
            for j in range(4):
                token_rows(f"ao{j}", tile(), oT2)
            pe.wait_ge(normed, 12)
            for k in range(4):
                turn(f"q2{k}", xn3, k)
            pe.wait_ge(sum_taken, NO["q23"] + 1)
            for j in range(2):
                token_rows(f"xq{j}", tile(), hT3)
            pe.wait_ge(qx_ready, 1)
            for k in range(2):
                turn(f"xqT{k}", qx, k)
            pe.wait_ge(sum_taken, NO["xqT1"] + 1)
            for n in range(XH + 2):
                if n < XH:
                    if n >= 2:
                        pe.wait_ge(probs, 3 * H2 + n - 1)
                    for j in range(NT):
                        mm = pe.matmul(bank[4 + n % 2][:, 256 * j:256 * j + 256], qxT[:, n, 128 * j:128 * j + 128],
                                       kxT[:, n, :], start=True, stop=True)
                    mm.then_inc(s_ready, 1)
                m = n - 1
                if 0 <= m < XH:
                    pe.wait_ge(probs, 3 * H2 + m + 1)
                    if m >= 2:
                        pe.wait_ge(pt_taken, 3 * H2 + m - 1)
                    for c in range(2):
                        for j in range(NT):
                            mm = pe.transpose(bank[6 + m % 2][:, 256 * c + 128 * j:256 * c + 128 * j + 128],
                                              xP[m % 2][:, 256 * j + 128 * c:256 * j + 128 * c + 128], ident)
                    mm.then_inc(pt_ready, 1)
                m = n - 2
                if m >= 0:
                    b = bank[m // 2]
                    pe.wait_ge(pt_taken, 3 * H2 + m + 1)
                    for j in range(NT):
                        for c in range(2):
                            mm = pe.matmul(b[:, 256 * (m % 2) + 128 * j:256 * (m % 2) + 128 * j + 128],
                                           xPT[m % 2][:, 256 * c + 128 * j:256 * c + 128 * j + 128],
                                           vx[:, c, XD * m:XD * m + XD], start=(c == 0), stop=(c == 1))
                    mm.then_inc(av_done, 1)
            pe.wait_ge(ox_ready, 2)
            for k in range(2):
                turn(f"oxT{k}", ox, k)
            pe.wait_ge(sum_taken, NO["oxT1"] + 1)
            for j in range(2):
                tile()
                w = ring[:, (t.n - 1) % RING, :].rearrange("p (k n) -> p k n", k=4)
                for i in range(NT):
                    b = fresh(f"xp{j}{i}")
                    for k in range(4):
                        mm = pe.matmul(b[:, :], oxT[:, k, 128 * i:128 * i + 128], w[:, k, :], start=(k == 0), stop=(k == 3))
                    mm.then_inc(sum_ready, 1)
            pe.wait_ge(normed, 14)
            for k in range(4):
                turn(f"q3{k}", xn3, k)
            pe.wait_ge(sum_taken, NO["q33"] + 1)
            for j in range(16):
                feature_rows(f"ff{j}", tile(), hT3)
            for q in range(16):
                tile()
                w = ring[:, (t.n - 1) % RING, :].rearrange("p (k n) -> p k n", k=2)
                pe.wait_ge(ff_ready, q + 1)
                for j in range(NT):
                    for n in range(2):
                        for k in range(2):
                            mm = pe.matmul(acc[2 * j + n][:, :], ffh[:, 2 * q + k, 128 * j:128 * j + 128],
                                           w[:, k, 512 * n:512 * n + 512], start=(q == 0 and k == 0), stop=(q == 15 and k == 1))
                mm.then_inc(ffo_done, 1)
            assert done.n == len(SUMS) and t.n == len(FREED)

        @block.vector
        def _(dve):
            step = Count()

            def W(ins):
                ins.then_inc(dve_step, 1)
                dve.wait_ge(dve_step, step.one())

            def root_means(n, when, many):
                dve.wait_ge(squares, when)
                dve.tensor_scalar(ms[:, 0:many], ss[:, 0:many], 1.0 / D, EPS, ALU.mult, ALU.add).then_inc(means, 1)
                dve.wait_ge(roots, n)
                dve.reciprocal(rs[:, 0:many], rt[:, 0:many]).then_inc(dve_step, 1)
                dve.wait_ge(dve_step, step.one())

            dve.wait_ge(mem_in, 16)
            root_means(1, 2, 2)
            for i in range(NT):
                dve.tensor_scalar(memx[:, i, :], memx[:, i, :], rs[:, i:i + 1], None, ALU.mult).then_inc(normed, 1)
            dve.wait_ge(x_in, 32)
            root_means(2, 6, 4)
            for i in range(4):
                dve.tensor_scalar(xr[:, i, :], xr[:, i, :], rs[:, i:i + 1], None, ALU.mult).then_inc(normed, 1)
            dve.wait_ge(sum_taken, NO["xk1"] + 1)
            k8 = kx.rearrange("p i (h e) -> p (i h) e", h=XH)
            W(dve.tensor_tensor(ksq, k8, k8, ALU.mult))
            W(dve.tensor_reduce(hms[:, 0:8], ksq, AX.X, ALU.add))
            dve.tensor_scalar(hms[:, 0:8], hms[:, 0:8], 1.0 / XD, EPS, ALU.mult, ALU.add).then_inc(head_ms, 1)
            dve.wait_ge(head_rt, 1)
            W(dve.reciprocal(hms[:, 0:8], hrt[:, 0:8]))
            dve.tensor_tensor(k8, k8, hms[:, 0:8].unsqueeze(2).broadcast_to([P, 8, XD]), ALU.mult).then_inc(kx_ready, 1)
            dve.memset(lrT[32:33, :], 1.0).then_inc(lr_ones, 1)
            dve.wait_ge(adaT_ready, 1)
            m1 = mod1[:, :].rearrange("p (k c) -> p k c", c=2)
            bias1 = cols[:, 0:16].unsqueeze(2).broadcast_to([P, 16, 2])
            turned1 = X[:, :].rearrange("p (b n g r) -> p b g n r", b=2, n=2, g=4)
            for b2 in range(2):
                dve.tensor_tensor(m1[:, 8 * b2:8 * b2 + 8, :].rearrange("p (g n) c -> p g n c", n=2),
                                  turned1[:, b2, :, :, 0:2],
                                  bias1[:, 8 * b2:8 * b2 + 8, :].rearrange("p (g n) c -> p g n c", n=2),
                                  ALU.add).then_inc(dve_step, 1)
                dve.wait_ge(dve_step, step.one())
            dve.scalar_tensor_tensor(m1[:, 8:16, :], m1[:, 8:16, :], 1.0,
                                     cols_of("norm_mix").unsqueeze(2).broadcast_to([P, 8, 2]),
                                     ALU.add, ALU.mult).then_inc(mod_ready, 1)
            for n in range(8):
                i, d = divmod(n, 2)
                name = f"z{i}{d}"
                nxt = {"wait": NO[name] + 1}
                dve.wait_ge(sum_taken, nxt["wait"])
                dve.wait_ge(act_step, 4 + 8 + 3 * n + 3)
                dve.tensor_tensor(la[:, i, d, :], la[:, i, d, :], spt[:, n % 2, :], ALU.add).then_inc(la_ready, 1)
            for d in range(2):
                for s in range(2):
                    dve.wait_ge(sum_taken, NO[f"e{d}{s}"] + 1)
                    dve.tensor_tensor(kd_g[:, d, s, :], kd_g[:, d, s, :], gkc[:, s, :], ALU.mult).then_inc(ctxk_ready, 1)
            dve.wait_ge(sum_taken, NO["rkc1"] + 1)
            kdec = C("kdec").rearrange("p (d s h) -> p d s h", d=2, s=2)
            for d in range(2):
                for s in range(2):
                    dve.tensor_tensor(kd_r[:, d, s, :].rearrange("p (h k) -> p h k", h=HEADS),
                                      rkc[:, s, :].rearrange("p (h k) -> p h k", h=HEADS),
                                      kdec[:, d, s, :].unsqueeze(2).broadcast_to([P, HEADS, DK]),
                                      ALU.mult).then_inc(ctxk_ready, 1)

            def gla_factors(h):
                dve.wait_ge(sum_taken, NO[f"fac{h}"] + 1)
                F = fac[h % 2].rearrange("p (d s) -> p d s", d=2)
                q2 = gq[:, h, :].unsqueeze(1).broadcast_to([P, 2, L])
                k2 = gk[:, h, :].unsqueeze(1).broadcast_to([P, 2, L])
                for at, m in ((0, q2), (256, k2), (512, q2)):
                    dve.tensor_tensor(F[:, :, at:at + 256], F[:, :, at:at + 256], m, ALU.mult).then_inc(dve_step, 1)
                    step.one()
                for d in range(2):
                    far, near = (128, 0) if d == 0 else (0, 128)
                    dve.tensor_tensor(F[:, d, 768:896], F[:, d, 768:896], gq[:, h, far:far + 128], ALU.mult).then_inc(dve_step, 1)
                    step.one()
                    last = dve.tensor_tensor(F[:, d, 896:1024], F[:, d, 896:1024], gk[:, h, near:near + 128], ALU.mult)
                    if d == 0:
                        last.then_inc(dve_step, 1)
                        step.one()
                    else:
                        last.then_inc(factors, 1)

            def ret_factors(i):
                h = i - HEADS
                f = fac[i % 2]
                qdec = C("qdec").rearrange("p (d h t) -> p d h t", d=2, h=HEADS)
                cs = C("cosf").unsqueeze(1).broadcast_to([P, 2, L])
                sn = C("sinf").unsqueeze(1).broadcast_to([P, 2, L])
                f2 = f[:, 0:512].rearrange("p (a b) -> p a b", a=2)
                dve.wait_ge(sum_taken, NO[f"fac{i}"] + 1)
                dve.tensor_tensor(rqk[:, h, :, :], rqk[:, h, :, :], cs, ALU.mult).then_inc(dve_step, 1)
                step.one()
                dve.tensor_tensor(f2, f2, sn, ALU.mult).then_inc(dve_step, 1)
                dve.wait_ge(dve_step, step.one())
                dve.tensor_tensor(f2, f2, rqk[:, h, :, :], ALU.add).then_inc(dve_step, 1)
                dve.wait_ge(dve_step, step.one())
                dve.tensor_tensor(f[:, 512:768], f[:, 0:256], qdec[:, 0, h, :], ALU.mult).then_inc(dve_step, 1)
                step.one()
                dve.tensor_tensor(f[:, 768:1024], f[:, 0:256], qdec[:, 1, h, :], ALU.mult).then_inc(factors, 1)

            mvv = mv[:, :].rearrange("p (h i c) -> p h i c", h=8, i=NT)
            gla_factors(0)
            for i in range(8):
                dve.wait_ge(scores, i + 1)
                if i >= 2:
                    dve.wait_ge(values, i - 1)
                s4 = scT[i % 2]
                if i < HEADS:
                    dve.tensor_copy(s4, X[:, :]).then_inc(dve_step, 1)
                    dve.wait_ge(dve_step, step.one())
                    up = C("upper").bitcast(U32)
                    dve.copy_predicated(s4[:, 0:128], up, Y[:, 0:128]).then_inc(dve_step, 1)
                    step.one()
                    dve.copy_predicated(s4[:, 384:512], up, Y[:, 128:256]).then_inc(scores_taken, 1)
                else:
                    h = i - HEADS
                    dve.tensor_tensor(s4, X[:, :], C("decay")[:, 512 * h:512 * h + 512], ALU.mult).then_inc(scores_taken, 1)
                if i + 1 < HEADS:
                    gla_factors(i + 1)
                elif i < 7:
                    ret_factors(i + 1)
                dve.wait_ge(values, i + 1)
                dve.wait_ge(sum_taken, NO[f"gate{i}"] + 1)
                for j in range(NT):
                    o = O[i % 2][:, 256 * j:256 * j + 256]
                    dve.bn_stats(stats[:, 6 * j:6 * j + 6], o).then_inc(dve_step, 1)
                    dve.wait_ge(dve_step, step.one())
                    dve.bn_aggr(mvv[:, i, j, :], stats[:, 6 * j:6 * j + 6]).then_inc(dve_step, 1)
                    dve.wait_ge(dve_step, step.one())
                    if i < HEADS:
                        last = dve.tensor_tensor(og[j][:, i, :], o, gate[i % 2][:, j, :], ALU.mult)
                    else:
                        last = dve.scalar_tensor_tensor(og[j][:, i, :], o, mvv[:, i, j, 0:1], gate[i % 2][:, j, :],
                                                        ALU.subtract, ALU.mult)
                    if j == 0:
                        last.then_inc(dve_step, 1)
                        step.one()
                    else:
                        last.then_inc(values_taken, 1)
            dve.wait_ge(values_taken, 8)
            hvv = hv[:, :].rearrange("p (h i) -> p h i", h=8)
            dve.tensor_tensor(hvv[:, 0:4, :], mvv[:, 0:4, :, 0], mvv[:, 0:4, :, 0], ALU.mult).then_inc(dve_step, 1)
            dve.wait_ge(dve_step, step.one())
            dve.tensor_tensor(hvv[:, 0:4, :], hvv[:, 0:4, :], mvv[:, 0:4, :, 1], ALU.add).then_inc(dve_step, 1)
            dve.wait_ge(dve_step, step.one())
            dve.tensor_copy(hvv[:, 4:8, :], mvv[:, 4:8, :, 1]).then_inc(dve_step, 1)
            dve.wait_ge(dve_step, step.one())
            dve.tensor_scalar(hv[:, :], hv[:, :], EPS, None, ALU.add).then_inc(head_var, 1)
            dve.wait_ge(head_root, 1)
            dve.reciprocal(hv[:, :], hr[:, :]).then_inc(dve_step, 1)
            dve.wait_ge(dve_step, step.one())
            for h in range(8):
                for j in range(NT):
                    dve.tensor_scalar(og[j][:, h, :], og[j][:, h, :], hvv[:, h, j:j + 1], None, ALU.mult).then_inc(og_ready, 1)
            dve.wait_ge(bias_in, 16)
            for n, name in enumerate(("g1a", "g1b", "g2a", "g2b")):
                dve.wait_ge(sum_taken, NO[name] + 1)
                g = region(V, 2048)[:, 512 * n:512 * n + 512]
                dve.tensor_tensor(g, g, tmp[n % 2], ALU.add).then_inc(gbc_ready, 1)
                if name == "g1b":
                    dve.wait_ge(sum_taken, NO["mod2"] + 1)
                    dve.tensor_tensor(mod2[:, :], mod2[:, :], cols[:, colat["b_sh2"][0]:colat["b_sh2"][0] + 16],
                                      ALU.add).then_inc(dve_step, 1)
                    dve.wait_ge(dve_step, step.one())
                    dve.scalar_tensor_tensor(mod2[:, 8:16], mod2[:, 8:16], 1.0, cols_of("norm_ffn"),
                                             ALU.add, ALU.mult).then_inc(mod2_ready, 1)
            n = 0
            for j in range(4):
                y = yT[:, 2 * j:2 * j + 2, :]
                for br in range(2):
                    dve.wait_ge(sum_taken, NO[("bg", "br")[br] + str(j)] + 1)
                    m = mT[:, 8 * br + 2 * j:8 * br + 2 * j + 2, :]
                    tv = tmp[n % 2].rearrange("p (a b) -> p a b", a=2)
                    if br == 0:
                        dve.tensor_tensor(y, tv, m, ALU.mult).then_inc(y_done, 1)
                    else:
                        dve.tensor_tensor(tv, tv, m, ALU.mult).then_inc(dve_step, 1)
                        dve.wait_ge(dve_step, step.one())
                        dve.tensor_tensor(y, y, tv, ALU.add).then_inc(y_done, 1)
                    n += 1
            dve.wait_ge(reload_in, 16)
            for j in range(4):
                dve.wait_ge(sum_taken, NO[f"wo{j}"] + 1)
                tv = tmp[n % 2].rearrange("p (a b) -> p a b", a=2)
                dve.tensor_tensor(tv, tv, g1bc[:, 256 * j:256 * j + 256].unsqueeze(1).broadcast_to([P, 2, 256]),
                                  ALU.mult).then_inc(dve_step, 1)
                dve.wait_ge(dve_step, step.one())
                hs = hlat[:, :, 256 * j:256 * j + 256]
                dve.tensor_tensor(hs, hs, tv, ALU.add).then_inc(res_done, 1)
                n += 1
            root_means(3, 8, 2)
            for i in range(NT):
                dve.tensor_scalar(xn2[:, i, :], hlat[:, i, :], rs[:, i:i + 1], None, ALU.mult).then_inc(normed, 1)
            dve.wait_ge(sum_taken, NO["rt"] + 1)
            V2 = [P, NT, 1]

            def S(ins):
                return ins.then_inc(dve_step, 1)

            def b2(v, n):
                return v.unsqueeze(2).broadcast_to([P, NT, n])

            dve.wait_ge(rows_in, 16)
            S(dve.tensor_tensor(lg, lg, row("router_b").unsqueeze(1).broadcast_to([P, NT, 36]), ALU.add))
            dve.wait_ge(dve_step, step.one())
            G = lg[:, :, 0:4]
            S(dve.tensor_reduce(r2[0], G, AX.X, ALU.max))
            dve.wait_ge(dve_step, step.one())
            dve.tensor_tensor(ge, G, b2(r2[0], 4), ALU.subtract).then_inc(rt_sub, 1)
            S(dve.tensor_tensor(sel, G, b2(r2[0], 4), ALU.is_equal))
            dve.wait_ge(dve_step, step.one())
            S(dve.tensor_tensor(sel, sel, C("tie4").unsqueeze(1).broadcast_to([P, NT, 4]), ALU.mult))
            dve.wait_ge(dve_step, step.one())
            S(dve.tensor_reduce(r2[1], sel, AX.X, ALU.max))
            dve.wait_ge(dve_step, step.one())
            S(dve.tensor_tensor(sel, sel, b2(r2[1], 4), ALU.is_equal))
            dve.wait_ge(dve_step, step.one())
            S(dve.tensor_scalar(sel, sel, -1.0, BIG, ALU.add, ALU.mult))
            dve.wait_ge(dve_step, step.one())
            for j in range(NT):
                S(dve.tensor_tensor(e1[:, j, :].rearrange("p (g e) -> p g e", g=4),
                                    lg[:, j, 4:36].rearrange("p (g e) -> p g e", g=4),
                                    sel[:, j, :].unsqueeze(2).broadcast_to([P, 4, 8]), ALU.add))
                step.one()
            dve.wait_ge(dve_step, step.n)

            def first_max(oh, vmax):
                S(dve.tensor_reduce(vmax, e1, AX.X, ALU.max))
                dve.wait_ge(dve_step, step.one())
                S(dve.tensor_tensor(oh, e1, b2(vmax, 32), ALU.is_equal))
                dve.wait_ge(dve_step, step.one())
                S(dve.tensor_tensor(oh, oh, C("tie32").unsqueeze(1).broadcast_to([P, NT, 32]), ALU.mult))
                dve.wait_ge(dve_step, step.one())
                S(dve.tensor_reduce(r2[2], oh, AX.X, ALU.max))
                dve.wait_ge(dve_step, step.one())
                S(dve.tensor_tensor(oh, oh, b2(r2[2], 32), ALU.is_equal))
                dve.wait_ge(dve_step, step.one())

            first_max(oh1, r2[3])
            S(dve.scalar_tensor_tensor(e1, oh1, -1e38, e1, ALU.mult, ALU.add))
            dve.wait_ge(dve_step, step.one())
            first_max(oh2, r2[4])
            dve.tensor_tensor(r2[5], r2[4], r2[3], ALU.subtract).then_inc(rt_dv, 1)
            dve.tensor_tensor(oh, oh1, oh2, ALU.add).then_inc(oh_ready, 1)
            dve.wait_ge(rt_exp, 1)
            S(dve.tensor_reduce(r2[7], ge, AX.X, ALU.add))
            dve.wait_ge(dve_step, step.one())
            dve.wait_ge(rt_ev, 1)
            S(dve.scalar_tensor_tensor(r2[8], r2[6], 1.0, r2[7], ALU.add, ALU.mult))
            dve.wait_ge(dve_step, step.one())
            S(dve.reciprocal(r2[9], r2[8]))
            dve.wait_ge(dve_step, step.one())
            S(dve.tensor_tensor(r2[10], r2[9], r2[6], ALU.mult))
            dve.wait_ge(dve_step, step.one())
            S(dve.tensor_tensor(oh1, oh1, b2(r2[9], 32), ALU.mult))
            step.one()
            S(dve.tensor_tensor(oh2, oh2, b2(r2[10], 32), ALU.mult))
            dve.wait_ge(dve_step, step.one())
            W(dve.memset(region(LC + 3584, 256), -1.0))
            W(dve.tensor_tensor(cw[:, :, 0:32], oh1, oh2, ALU.add))
            dve.wait_ge(sum_taken, NO["rank"] + 1)
            W(dve.scalar_tensor_tensor(pos[:, :, 0:32], rank[:, 0:2, 0:32], 1.0, oh, ALU.add, ALU.mult))
            W(dve.tensor_scalar(pos[:, :, 0:32], pos[:, :, 0:32], -1.0, None, ALU.add))
            W(dve.tensor_reduce(r2[11][:, 0:1], rank[:, 2, 0:32], AX.X, ALU.max))
            dve.tensor_scalar(over_i[:, :], r2[11][:, 0:1], float(CAP), None, ALU.is_gt).then_inc(over_ready, 1)
            slots = C("slots").unsqueeze(1).broadcast_to([P, 2, CAP])

            def experts(R, r, first):
                def per_expert(v, j, e):
                    return v[:, j, bass.ds(e, 2)].unsqueeze(2).broadcast_to([P, 2, CAP])

                def places(e, n):
                    for j in range(NT):
                        ins = dve.tensor_tensor(Pm[:, j, :].rearrange("p (e c) -> p e c", e=2), per_expert(pos, j, e),
                                                slots, ALU.is_equal)
                        if j == 1:
                            ins.then_inc(R.p_ready, 1)
                            dve.wait_ge(R.p_ready, n)

                if not first:
                    dve.wait_ge(R.added, r + 1)
                    dve.tensor_scalar(pos, pos, -float(CAP), None, ALU.add).then_inc(moved, 1)
                    dve.wait_ge(moved, r + 1)
                dve.memset(hT_PT, 0.0).then_inc(R.y_taken, 1)
                dve.memset(ysb, 0.0).then_inc(R.y_taken, 1)
                places(0, r * (PAIRS + 1) + 1)
                if first:
                    dve.memset(hid, 0.0).then_inc(acc_open, 1)
                dve.memset(sil, 0.0).then_inc(R.hid_ready, 1)
                with dve.Fori(0, PAIRS) as i:
                    for j in range(NT):
                        ins = dve.tensor_tensor(Pw[:, j, :].rearrange("p (e c) -> p e c", e=2),
                                                Pm[:, j, :].rearrange("p (e c) -> p e c", e=2), per_expert(cw, j, i * 2),
                                                ALU.mult)
                    ins.then_inc(R.pw_ready, 1)
                    dve.wait_ge(R.pw_ready, r * PAIRS + (i + 1))
                    dve.wait_ge(R.xg_taken, r * (2 * PAIRS + 2) + (i * 2 + 2))
                    places(i * 2 + 2, r * (PAIRS + 1) + (i + 2))
                    dve.wait_ge(R.u_done, r * PAIRS + (i + (1 + R.ahead)))
                    dve.wait_ge(R.sil_ready, r * PAIRS + (i + 1))
                    dve.tensor_tensor(hid, sil, bank[0][:, FF:2 * FF], ALU.mult).then_inc(R.hid_ready, 1)
                    for n in range(2):
                        dve.wait_ge(R.y_ready, r * (2 * PAIRS) + (i * 2 + (n + 1 + 2 * R.ahead)))
                        dve.tensor_copy(ysb[:, 512 * n:512 * n + 512], bank[1 + n][:, :]).then_inc(R.y_taken, 1)

            experts(main, 0, True)
            over = dve.value_load(over_i[0:1, 0:1], min_val=0, max_val=1)
            with dve.If(over > 0):
                dve.wait_ge(main.added, 1)
                dve.memset(sil, 0.0).then_inc(more.added, 1)
                with dve.Fori(0, L // CAP - 1) as r:
                    experts(more, r, False)
                dve.wait_ge(more.added, L // CAP)
            dve.wait_ge(main.added, 1)
            for j in range(NT):
                for n in range(2):
                    tv = tmp[n]
                    S(dve.tensor_tensor(tv, acc[2 * j + n][:, :], g2bc[:, 512 * n:512 * n + 512], ALU.mult))
                    dve.wait_ge(dve_step, step.one())
                    hs = hlat[:, j, 512 * n:512 * n + 512]
                    dve.tensor_tensor(hs, hs, tv, ALU.add).then_inc(moe_done, 1)
                    dve.wait_ge(moe_done, 2 * j + n + 1)
            root_means(4, 10, 2)
            dve.wait_ge(nfin_in, 16)
            for i in range(NT):
                dve.scalar_tensor_tensor(hlat[:, i, :], hlat[:, i, :], rs[:, i:i + 1], g1bc, ALU.mult, ALU.mult).then_inc(x2_ready, 1)
            dve.wait_ge(x2_ready, 2)
            root_means(5, 12, 2)
            for i in range(NT):
                dve.tensor_scalar(xn2[:, i, :], hlat[:, i, :], rs[:, i:i + 1], None, ALU.mult).then_inc(normed, 1)

            dve.wait_ge(sum_taken, NO["pj6"] + 1)
            W(dve.tensor_tensor(cq, p2[:, :, 0:384], p2[:, :, 0:384], ALU.mult))
            m4 = hms[:, 0:4].rearrange("p (i c) -> p i c", c=2)
            W(dve.tensor_reduce(m4[:, :, 0:1], cq[:, :, 0:256], AX.X, ALU.add))
            W(dve.tensor_reduce(m4[:, :, 1:2], cq[:, :, 256:384], AX.X, ALU.add))
            W(dve.tensor_scalar(m4[:, :, 0:1], m4[:, :, 0:1], 1.0 / 256, EPS, ALU.mult, ALU.add))
            dve.tensor_scalar(m4[:, :, 1:2], m4[:, :, 1:2], 1.0 / 128, EPS, ALU.mult, ALU.add).then_inc(head_ms, 1)
            dve.wait_ge(head_rt, 2)
            W(dve.reciprocal(hms[:, 0:4], hrt[:, 0:4]))
            W(dve.tensor_tensor(cq[:, :, 0:256], p2[:, :, 0:256], m4[:, :, 0:1].broadcast_to([P, NT, 256]), ALU.mult))
            dve.tensor_tensor(cq[:, :, 256:384], p2[:, :, 256:384], m4[:, :, 1:2].broadcast_to([P, NT, 128]),
                              ALU.mult).then_inc(cT_ready, 1)
            dve.wait_ge(sum_taken, NO["kb"] + 1)
            pe_cols = cols_of("pe").rearrange("p (c l) -> p c l", c=2)
            for kv in range(2):
                kv16 = kbT[:, kv, :].rearrange("p (m l) -> p l m", l=16)
                for a in range(2):
                    dve.tensor_tensor(BL[:, kv, 16 * a:16 * a + 16, :], kv16[:, :, a:a + NCMP],
                                      pe_cols[:, kv, 16 * a:16 * a + 16].unsqueeze(2).broadcast_to([P, 16, NCMP]),
                                      ALU.add).then_inc(bl_ready, 1)
            W(dve.tensor_scalar(wsc, p2[:, :, 448:456], IDX_SCALE, None, ALU.mult))
            W(dve.tensor_copy(R[:, :, 8:16, :].rearrange("p i h e -> p i (h e)"), p2[:, :, 456:968]))
            for br in range(2):
                at = KV0 + 256 * (br + 1)
                W(dve.tensor_copy(R[:, :, 26 + 4 * br:30 + 4 * br:2, :],
                                  p2[:, :, at:at + 128].rearrange("p i (g e) -> p i g e", g=2)))
            for i in range(NT):
                W(dve.bn_stats(stats[:, 6 * i:6 * i + 6], p2[:, i, 384:448]))
                W(dve.bn_aggr(mvv[:, 0, i, :], stats[:, 6 * i:6 * i + 6]))
            W(dve.tensor_scalar(hms[:, 42:44], mvv[:, 0, :, 1], EPS, None, ALU.add))
            dve.wait_ge(sum_taken, NO["kvd"] + 1)
            for i in range(NT):
                W(dve.tensor_tensor(sqa[:, i, :, :], R[:, i, 0:16, :], R[:, i, 0:16, :], ALU.mult))
                W(dve.tensor_tensor(sqb[:, i, :, :], R[:, i, 24:34:2, :], R[:, i, 24:34:2, :], ALU.mult))
            W(dve.tensor_reduce(hms[:, 0:32], sqa.rearrange("p i h e -> p (i h) e"), AX.X, ALU.add))
            W(dve.tensor_reduce(hms[:, 32:42], sqb.rearrange("p i h e -> p (i h) e"), AX.X, ALU.add))
            dve.tensor_scalar(hms[:, 0:42], hms[:, 0:42], 1.0 / HD, EPS, ALU.mult, ALU.add).then_inc(head_ms, 1)
            dve.wait_ge(sum_taken, NO["cv1"] + 1)
            W(dve.tensor_tensor(kr[0:NCMP], KC[0:NCMP], KC[0:NCMP], ALU.mult))
            W(dve.tensor_reduce(hms[0:NCMP, 44:46], kr[0:NCMP], AX.X, ALU.add))
            dve.tensor_scalar(hms[0:NCMP, 44:46], hms[0:NCMP, 44:46], 1.0 / HD, EPS, ALU.mult, ALU.add).then_inc(head_ms, 1)
            dve.wait_ge(head_rt, 3)
            W(dve.reciprocal(hms[:, 0:44], hrt[:, 0:44]))
            W(dve.tensor_scalar(hms[:, 0:32], hms[:, 0:32], HD ** -0.5, None, ALU.mult))
            for i in range(NT):
                W(dve.tensor_tensor(R[:, i, 0:16, :], R[:, i, 0:16, :],
                                    hms[:, 16 * i:16 * i + 16].unsqueeze(2).broadcast_to([P, 16, HD]), ALU.mult))
                W(dve.tensor_tensor(R[:, i, 24:34:2, :], R[:, i, 24:34:2, :],
                                    hms[:, 32 + 5 * i:37 + 5 * i].unsqueeze(2).broadcast_to([P, 5, HD]), ALU.mult))
                for a, z, st2, gain in ((0, 8, 1, "dsa_qn"), (8, 16, 1, "nsa_qn"), (24, 25, 1, "dsa_kn"),
                                        (26, 30, 2, "kn_slc"), (30, 34, 2, "kn_win")):
                    hs = R[:, i, a:z:st2, :]
                    nh = len(range(a, z, st2))
                    W(dve.tensor_tensor(hs, hs, row(gain).unsqueeze(1).broadcast_to([P, nh, HD]), ALU.mult))
                ki = R[:, i, 34, :]
                W(dve.tensor_scalar(ki, p2[:, i, 384:448], mvv[:, 0, i, 0:1], hms[:, 42 + i:43 + i], ALU.subtract, ALU.mult))
                W(dve.tensor_tensor(ki, ki, row("idx_g"), ALU.mult))
                W(dve.tensor_tensor(ki, ki, row("idx_b"), ALU.add))

            def rotate(src, dsts, cos, sin, parts, nh):
                a = t1[0:parts, 0:32 * nh].rearrange("p (h e) -> p h e", e=32)
                b = t2[0:parts, 0:32 * nh].rearrange("p (h e) -> p h e", e=32)
                cb = cos[0:parts].unsqueeze(1).broadcast_to([parts, nh, 32])
                sb_ = sin[0:parts].unsqueeze(1).broadcast_to([parts, nh, 32])
                x1, x2 = src[:, :, 0:32], src[:, :, 32:64]
                for half, (u, v, op) in enumerate(((x1, x2, ALU.subtract), (x2, x1, ALU.add))):
                    S(dve.tensor_tensor(a, u, cb, ALU.mult))
                    step.one()
                    W(dve.tensor_tensor(b, v, sb_, ALU.mult))
                    for dst in dsts:
                        W(dve.tensor_tensor(dst[:, :, 32 * half:32 * half + 32], a, b, op))

            dve.wait_ge(head_rt, 4)
            W(dve.reciprocal(hms[0:NCMP, 44:46], hrt[0:NCMP, 44:46]))
            W(dve.tensor_tensor(KC[0:NCMP], KC[0:NCMP], hms[0:NCMP, 44:46].unsqueeze(2).broadcast_to([NCMP, 2, HD]), ALU.mult))
            W(dve.tensor_tensor(KC[0:NCMP], KC[0:NCMP],
                                row("kn_cmp")[0:NCMP].unsqueeze(1).broadcast_to([NCMP, 2, HD]), ALU.mult))
            rotate(KC[0:NCMP], [KCD[0:NCMP, :, 0, :], KCD[0:NCMP, :, 1, :]], C("cosc"), C("sinc"), NCMP, 2)
            dve.memset(ss[:, 3:4], 0.0).then_inc(kc_ready, 1)
            dve.wait_ge(kc_ready, 1)
            for i in range(NT):
                cs, sn = C("cos2")[:, 32 * i:32 * i + 32], C("sin2")[:, 32 * i:32 * i + 32]
                rotate(R[:, i, 0:24, :], [R2[:, i, 0:24, :]], cs, sn, P, 24)
                rotate(R[:, i, 24:36:2, :], [R2[:, i, 24:36:2, :], R2[:, i, 25:36:2, :]], cs, sn, P, 6)
            dve.memset(cS, 0.0).then_inc(heads_ready, 1)
            for h in range(H2):
                dve.wait_ge(idx_relu, h + 1)
                for i, (a, z) in enumerate(((0, 128), (128, 384))):
                    w = wsc[:, i, h:h + 1]
                    if h == 0:
                        ins = dve.tensor_scalar(iacc[:, a:z], rel[0][:, a:z], w, None, ALU.mult)
                    else:
                        ins = dve.scalar_tensor_tensor(iacc[:, a:z], rel[h % 2][:, a:z], w, iacc[:, a:z], ALU.mult, ALU.add)
                    if i == 0:
                        S(ins)
                        step.one()
                    else:
                        ins.then_inc(idx_taken, 1)
                        dve.wait_ge(idx_taken, h + 1)
            W(dve.tensor_tensor(iacc, iacc, C("causal"), ALU.add))
            dve.wait_ge(heads_ready, 1)
            dve.wait_ge(cs_ready, 2)
            c16 = cS.rearrange("p (g n) -> p g n", n=16)[:, :, 0:NCMP]
            cm = C("cmask").rearrange("p (i n) -> p i n", i=NT)
            for par in range(2):
                for i in range(NT):
                    at = 8 * par + 4 * i
                    W(dve.tensor_tensor(c16[:, at:at + 4, :],
                                        bank[6 + par][:, 64 * i:64 * i + 64].rearrange("p (h n) -> p h n", n=16)[:, :, 0:NCMP],
                                        cm[:, i, :].unsqueeze(1).broadcast_to([P, 4, NCMP]), ALU.add))
            W(dve.tensor_reduce(cmx, c16, AX.X, ALU.max))
            W(dve.tensor_scalar(cmx, cmx, -BIG / 10, None, ALU.max))
            dve.tensor_tensor(c16, c16, cmx.unsqueeze(2).broadcast_to([P, 16, NCMP]), ALU.subtract).then_inc(cs_sub, 1)
            dve.wait_ge(cs_exp, 1)
            W(dve.tensor_reduce(crs, c16, AX.X, ALU.add))
            W(dve.tensor_scalar(crs, crs, 1e-30, None, ALU.max))
            W(dve.reciprocal(crs, crs))
            dve.wait_ge(gates_ready, 1)
            c4 = crs.rearrange("p (a i h) -> p a i h", a=2, i=NT)
            for par in range(2):
                W(dve.tensor_tensor(c4[:, par, :, :], c4[:, par, :, :], gates[:, :, par:8:2, 0], ALU.mult))
            for i in range(NT):
                dve.wait_ge(sum_taken, NO[f"co{i}"] + 1)
                for par in range(2):
                    W(dve.tensor_tensor(OA[:, i, 512:1024].rearrange("p (h a e) -> p a h e", a=2, e=HD)[:, par, :, :],
                                        tm[i].rearrange("p (h a e) -> p a h e", a=2, e=HD)[:, par, :, :],
                                        c4[:, par, i, :].unsqueeze(2).broadcast_to([P, 4, HD]), ALU.mult))
            dve.memset(ss[:, 3:4], 0.0).then_inc(o_taken, 1)

            def pick(n):
                k, i = divmod(n, NT)
                a, z = ((0, 128), (128, 384))[i]
                W(dve.max(top8[:, 8 * i:8 * i + 8], iacc[:, a:z]))
                W(dve.match_replace(iacc[:, a:z], top8[:, 8 * i:8 * i + 8], iacc[:, a:z], -3e38))

            def finish(g):
                dve.wait_ge(o_read, g + 1)
                T = tm[g % 2].rearrange("p (i h e) -> p i h e", i=NT, h=4)
                r = ssum[:, 8 * (g % 2):8 * (g % 2) + 8].rearrange("p (i h) -> p i h", i=NT)
                W(dve.reciprocal(r, r))
                h0 = 4 * (g % 2)
                if g < 4:
                    W(dve.tensor_tensor(r, r, gates[:, :, h0:h0 + 4, 1 + g // 2], ALU.mult))
                at = (512 if g < 4 else 0) + HD * h0
                for i in range(NT):
                    o = OA[:, i, at:at + 256].rearrange("p (h e) -> p h e", h=4)
                    rb = r[:, i, :].unsqueeze(2).broadcast_to([P, 4, HD])
                    if g < 4:
                        W(dve.tensor_tensor(T[:, i, :, :], T[:, i, :, :], rb, ALU.mult))
                        ins = dve.tensor_tensor(o, o, T[:, i, :, :], ALU.add)
                    else:
                        ins = dve.tensor_tensor(o, T[:, i, :, :], rb, ALU.mult)
                    if i == 0:
                        W(ins)
                    else:
                        ins.then_inc(o_taken, 1)

            for n in range(3 * H2):
                dve.wait_ge(s_ready, n + 1)
                if n >= 3:
                    dve.wait_ge(pt_ready, n - 2)
                mask = C("causal") if n < 2 * H2 else ibias
                W(dve.tensor_tensor(sS[n % 3], bank[4 + n % 2][:, 0:384], mask, ALU.add))
                for i, (a, z) in enumerate(((0, 128), (128, 384))):
                    dve.tensor_reduce(smx[:, 2 * (n % 4) + i:2 * (n % 4) + i + 1], sS[n % 3][:, a:z], AX.X, ALU.max,
                                      negate=True).then_inc((dve_step, s_max)[i], 1)
                step.one()
                if n < 2 * H2:
                    pick(n)
                if n == 2 * H2 - 1:
                    W(dve.tensor_scalar(ibias, iacc, -2e38, -BIG, ALU.is_gt, ALU.mult))
                    W(dve.tensor_tensor(ibias, ibias, C("causal"), ALU.add))
                if n >= 8 and n % 4 == 0:
                    finish(n // 4 - 2)
            finish(4)
            dve.wait_ge(o_taken, 6)
            finish(5)
            n = 0
            for j in range(4):
                dve.wait_ge(sum_taken, NO[f"ao{j}"] + 1)
                hs = hlat[:, :, 256 * j:256 * j + 256]
                dve.tensor_tensor(hs, hs, tm[j % 2].rearrange("p (a b) -> p a b", a=2), ALU.add).then_inc(x1_done, 1)
            root_means(6, 14, 2)
            for i in range(NT):
                dve.tensor_scalar(xn3[:, i, :], hlat[:, i, :], rs[:, i:i + 1], None, ALU.mult).then_inc(normed, 1)
            dve.wait_ge(sum_taken, NO["xq1"] + 1)
            q8 = qx.rearrange("p i (h e) -> p (i h) e", h=XH)
            W(dve.tensor_tensor(qsq, q8, q8, ALU.mult))
            W(dve.tensor_reduce(hms[:, 0:8], qsq, AX.X, ALU.add))
            dve.tensor_scalar(hms[:, 0:8], hms[:, 0:8], 1.0 / XD, EPS, ALU.mult, ALU.add).then_inc(head_ms, 1)
            dve.wait_ge(head_rt, 5)
            W(dve.reciprocal(hms[:, 0:8], hrt[:, 0:8]))
            dve.tensor_tensor(q8, q8, hms[:, 0:8].unsqueeze(2).broadcast_to([P, 8, XD]), ALU.mult).then_inc(qx_ready, 1)
            for n in range(XH):
                dve.wait_ge(s_ready, 3 * H2 + n + 1)
                W(dve.tensor_reduce(smx[:, 2 * n:2 * n + 2], bank[4 + n % 2][:, :].rearrange("p (i m) -> p i m", i=NT),
                                    AX.X, ALU.max, negate=True))
                dve.tensor_scalar(smx[:, 2 * n:2 * n + 2], smx[:, 2 * n:2 * n + 2], XD ** -0.5, None,
                                  ALU.mult).then_inc(s_max, 1)
            dve.wait_ge(probs, 3 * H2 + XH)
            W(dve.reciprocal(ssum[:, 0:8], ssum[:, 0:8]))
            rx = ssum[:, 0:8].rearrange("p (i h) -> p h i", i=NT)
            for k in range(2):
                dve.wait_ge(o_read, 6 + k + 1)
                dve.tensor_tensor(ox[:, :, 256 * k:256 * k + 256].rearrange("p i (h e) -> p h i e", h=2),
                                  tm[k].rearrange("p (h i e) -> p h i e", h=2, i=2),
                                  rx[:, 2 * k:2 * k + 2, :].unsqueeze(3).broadcast_to([P, 2, 2, XD]),
                                  ALU.mult).then_inc(ox_ready, 1)
            for n in range(4):
                j, i = divmod(n, 2)
                dve.wait_ge(sum_taken, NO[f"xp{j}{i}"] + 1)
                hs = hlat[:, i, 512 * j:512 * j + 512]
                dve.tensor_tensor(hs, hs, tm[n % 2], ALU.add).then_inc(x1_done, 1)
            root_means(7, 16, 2)
            for i in range(NT):
                dve.tensor_scalar(xn3[:, i, :], hlat[:, i, :], rs[:, i:i + 1], None, ALU.mult).then_inc(normed, 1)
            for j in range(16):
                dve.wait_ge(sum_taken, NO[f"ff{j}"] + 1)
                f = ffh[:, 2 * j:2 * j + 2, :]
                dve.tensor_tensor(f, f, f, ALU.mult).then_inc(ff_ready, 1)
            dve.wait_ge(ffo_done, 16)
            for n in range(4):
                hs = hlat[:, n // 2, 512 * (n % 2):512 * (n % 2) + 512]
                dve.tensor_tensor(hs, hs, acc[n][:, :], ALU.add).then_inc(x_final, 1)


def column_tile(w, at, width=TC):
    t = np.zeros((P, KD, TC), w.dtype)
    t[:, :, :width] = w[:, at:at + width].reshape(KD, P, width).transpose(1, 0, 2)
    return t.reshape(P, TW)


def row_tile(w, at):
    return w[at:at + 256].reshape(2, P, 1024).transpose(1, 0, 2).reshape(P, TW)


def stream_of(a):
    ada, win = a["w_ada"][0], a["w_in"][0]
    s = [column_tile(a["w_xk_2"][0], 256 * j) for j in range(2)]
    s += [column_tile(a["w_xv_2"][0], 256 * j) for j in range(2)]
    s += [column_tile(ada, 256 * n) for n in range(8)]
    s.append(column_tile(win, 3072, 32))
    gqa, gka, gva, gga, rqa, rka, rva, rga, mga = 0, 512, 1024, 2048, 3104, 3616, 4128, 5152, 6176
    s += [column_tile(win, gka + 256 * j) for j in range(2)]
    s += [column_tile(win, gva + 256 * j) for j in range(4)]
    s += [column_tile(win, gqa + 256 * j) for j in range(2)]
    s += [column_tile(win, rka + 256 * j) for j in range(2)]
    s += [column_tile(win, rva + 256 * j) for j in range(4)]
    s += [column_tile(win, rqa + 256 * j) for j in range(2)]
    for i in range(8):
        s.append(column_tile(win, gga + 256 * i if i < 4 else rga + 256 * (i - 4)))
        s.append(column_tile(win, mga + 256 * i))
    s += [column_tile(ada, 256 * n) for n in range(8, 24)]
    for j in range(4):
        s.append(column_tile(a["w_branch_gla"][0], 256 * j))
        s.append(column_tile(a["w_branch_ret"][0], 256 * j))
    s += [column_tile(a["w_out"][0], 256 * j) for j in range(4)]
    for i in range(PAIRS):
        for name, cut in (("w_expert_gate", column_tile), ("w_expert_up", column_tile), ("w_expert_down", row_tile)):
            s += [cut(a[name][0, 2 * i + e], 0) for e in range(2)]
    win2 = np.zeros((D, 1792), np.float32)
    win2[:, :1760] = a["w_in_2"][0]
    s += [column_tile(win2, 256 * j) for j in range(7)]
    s.append(row_tile(np.concatenate([a["w_dsa_uq_2"][0], a["w_idx_q_2"][0]], 1), 0))
    for kv in range(2):
        w = a["w_nsa_cmp_2"][0, kv].transpose(1, 0, 2).reshape(HD, TW)
        s.append(np.concatenate([w, w], 0))
    s += [column_tile(a["w_out_2"][0], 256 * j) for j in range(4)]
    s += [column_tile(a["w_xq_2"][0], 256 * j) for j in range(2)]
    for j in range(2):
        s.append(a["w_xo_2"][0][:, 512 * j:512 * j + 512].reshape(4, P, 512).transpose(1, 0, 2).reshape(P, TW))
    s += [column_tile(a["w_ff_in_2"][0], 256 * j) for j in range(16)]
    s += [row_tile(a["w_ff_out_2"][0], 256 * j) for j in range(16)]
    assert len(s) == len(FREED)
    return np.stack(s)


def layouts(a):
    def cl(v):
        return np.asarray(v).reshape(-1, P).T

    ba = a["b_ada"][0]
    cols = np.concatenate([cl(ba[0:1024]), cl(ba[1024:2048]), cl(a["norm_mix"][0]), cl(ba[3072:4096]),
                           cl(ba[4096:5120]), cl(a["norm_ffn"][0]), cl(a["gla_norm"][0]), cl(a["norm1_g_2"][0]),
                           cl(a["norm2_g_2"][0]), cl(a["mem_norm_g_2"][0]), cl(a["norm3_g_2"][0]),
                           cl(a["dsa_cq_g_2"][0]), cl(a["dsa_ckv_g_2"][0]), cl(a["xq_norm_g_2"][0]),
                           cl(a["xk_norm_g_2"][0]),
                           np.concatenate([a["nsa_cmp_pe_2"][0].transpose(2, 0, 1).reshape(HD, 64)] * 2, 0)], 1)
    rows = np.concatenate([a["b_router_group"][0], a["b_router_expert"][0], a["dsa_qn_g_2"][0], a["nsa_qn_g_2"][0],
                           a["dsa_kn_g_2"][0], a["nsa_kn_g_2"][0, 1], a["nsa_kn_g_2"][0, 2], a["idx_k_ln_g_2"][0],
                           a["idx_k_ln_b_2"][0], a["nsa_kn_g_2"][0, 0]])
    bias = np.concatenate([ba[2048:3072], ba[5120:6144], a["norm_final"]])
    cvec = np.stack([cl(a["c"][0]), cl(a["c_ctx"])], 2).reshape(P, KD * 2)
    wlr = np.zeros((33, 1024), np.float32)
    wlr[0:16, 0:512] = a["gla_lr_w"][0, 0]
    wlr[16:32, 512:1024] = a["gla_lr_w"][0, 1]
    wlr[32, 0:512] = a["gla_lr_b"][0, 0]
    wlr[32, 512:1024] = a["gla_lr_b"][0, 1]
    wr = np.concatenate([a["w_router_group"][0], a["w_router_expert"][0]], 1).reshape(KD, P, 36)
    return {"stream": stream_of(a), "consts": constants(), "cols": cols, "rows": rows, "bias": bias,
            "x": a["x"], "ctx": a["ctx"], "cvec": cvec, "wlr": wlr,
            "wr": wr.transpose(1, 0, 2).reshape(P, KD * 36), "mem": a["mem_2"], "wukv": a["w_dsa_ukv_2"][0]}


def kernel(**inputs):
    import concourse.bacc as bacc
    from concourse.bass_utils import run_bass_kernel_spmd as run

    a = {k: np.asarray(v) for k, v in inputs.items()}
    arrays = {k: np.ascontiguousarray(v) for k, v in layouts(a).items()}
    nc = bacc.Bacc("TRN2", target_bir_lowering=False, num_devices=1)
    aps = [nc.dram_tensor("in_" + k, v.shape, mybir.dt.from_np(v.dtype), kind="ExternalInput").ap()
           for k, v in arrays.items()]
    out = nc.dram_tensor("out", (1, L, D), F32, kind="ExternalOutput").ap()
    program(nc, *aps, out)
    r = run(nc, [{"in_" + k: v for k, v in arrays.items()}], core_ids=[0])
    return r.results[0]["out"]
```
